# Optimizing a Trainium2 kernel written in Bass

```python
import jax, jax.numpy as jnp
from jax import lax
import numpy as np

D_MODEL = 1024
BATCH = 1
SEQ = 512
DEPTH = 1
DEC_BATCH = 1
DEC_SEQ = 64
PAST_LEN = 128

CHUNK = 64
N_LEFT_CHUNKS = 8
LEFT_CTX = N_LEFT_CHUNKS * CHUNK
ATT_HEADS = 8
HEAD_DIM = 64
ATT_DIM = ATT_HEADS * HEAD_DIM
REL_CLIP = 128
N_REL = 2 * REL_CLIP + 1
CONV_DIM = D_MODEL // 2
CONV_WIDTH = 3
PEER_HEADS = 8
PEER_NKEYS = 128
PEER_N = PEER_NKEYS * PEER_NKEYS
PEER_DKEY = 256
PEER_HALF = PEER_DKEY // 2
PEER_TOPK = 16
PEER_BLOCK = 128
EPS = 1e-6
IN_COLS = 3 * ATT_DIM + 3 * CONV_DIM + 2 * D_MODEL
IN_SPLITS = (ATT_DIM, 2 * ATT_DIM, 3 * ATT_DIM,
             3 * ATT_DIM + CONV_DIM, 3 * ATT_DIM + 2 * CONV_DIM, 3 * ATT_DIM + 3 * CONV_DIM,
             3 * ATT_DIM + 3 * CONV_DIM + D_MODEL)

kernel_name = "hybrid_stream_bandattn_shortconv_peer_step"

def rms_norm(x, gain):
    xf = x.astype(jnp.float32)
    y = xf * lax.rsqrt(jnp.mean(xf * xf, axis=-1, keepdims=True) + EPS)
    return (y * gain.astype(jnp.float32)).astype(x.dtype)

def adaln(c, w_ada, b_ada):
    mod = jax.nn.silu(c) @ w_ada + b_ada
    return jnp.split(mod[:, None, :], 6, axis=-1)

def rel_bias(rel_table, n_q, n_k, offset):
    dist = jnp.arange(n_q)[:, None] + offset - jnp.arange(n_k)[None, :]
    idx = jnp.clip(dist, -REL_CLIP, REL_CLIP) + REL_CLIP
    return rel_table[:, idx]

def band_softmax_attend(q, k, v, bias, valid):
    s = jnp.einsum("bqhd,bkhd->bhqk", q, k).astype(jnp.float32) * (HEAD_DIM ** -0.5)
    s = s + bias.astype(jnp.float32)
    s = jnp.where(valid, s, -1e30)
    p = jax.nn.softmax(s, axis=-1).astype(v.dtype)
    return jnp.einsum("bhqk,bkhd->bqhd", p, v)

def prompt_band_attention(q, k, v, rel_table):
    B, S = q.shape[0], q.shape[1]
    n_chunks = S // CHUNK
    band = LEFT_CTX + CHUNK
    pad = jnp.zeros((B, LEFT_CTX, ATT_HEADS, HEAD_DIM), k.dtype)
    k_pad = jnp.concatenate([pad, k], axis=1)
    v_pad = jnp.concatenate([pad.astype(v.dtype), v], axis=1)
    bias = rel_bias(rel_table, CHUNK, band, LEFT_CTX)

    def one_chunk(n):
        start = n * CHUNK
        q_c = lax.dynamic_slice_in_dim(q, start, CHUNK, axis=1)
        k_b = lax.dynamic_slice_in_dim(k_pad, start, band, axis=1)
        v_b = lax.dynamic_slice_in_dim(v_pad, start, band, axis=1)
        valid = jnp.arange(band) >= LEFT_CTX - start
        return band_softmax_attend(q_c, k_b, v_b, bias, valid)

    out = lax.map(one_chunk, jnp.arange(n_chunks))
    return jnp.moveaxis(out, 0, 1).reshape(B, S, ATT_DIM)

def sample_band_attention(q, k_new, v_new, cache_k, cache_v, rel_table):
    B, T = q.shape[0], q.shape[1]
    k_all = jnp.concatenate([cache_k.astype(k_new.dtype), k_new], axis=1)
    v_all = jnp.concatenate([cache_v.astype(v_new.dtype), v_new], axis=1)
    n_past = cache_k.shape[1]
    bias = rel_bias(rel_table, T, k_all.shape[1], n_past)
    valid = jnp.ones((k_all.shape[1],), dtype=bool)
    return band_softmax_attend(q, k_all, v_all, bias, valid).reshape(B, T, ATT_DIM)

def causal_short_conv(u, buf, conv_w):
    T = u.shape[1]
    full = jnp.concatenate([buf.astype(u.dtype), u], axis=1)
    y = full[:, 0:T] * conv_w[0]
    for j in range(1, CONV_WIDTH):
        y = y + full[:, j:j + T] * conv_w[j]
    return y, full[:, -(CONV_WIDTH - 1):]

def peer_channel_mixer(h, w_pq, sub_keys1, sub_keys2, expert_u, expert_v):
    lead = h.shape[:-1]
    hf = h.reshape(-1, D_MODEL)
    n = hf.shape[0]
    n_pad = (-n) % PEER_BLOCK
    blocks = jnp.pad(hf, ((0, n_pad), (0, 0))).reshape(-1, PEER_BLOCK, D_MODEL)

    def one_block(hb):
        q = (hb @ w_pq).reshape(PEER_BLOCK, PEER_HEADS, 2, PEER_HALF)
        s1 = jnp.einsum("thd,hkd->thk", q[:, :, 0], sub_keys1).astype(jnp.float32)
        s2 = jnp.einsum("thd,hkd->thk", q[:, :, 1], sub_keys2).astype(jnp.float32)
        v1, i1 = lax.top_k(s1, PEER_TOPK)
        v2, i2 = lax.top_k(s2, PEER_TOPK)
        cand = (v1[..., :, None] + v2[..., None, :]).reshape(PEER_BLOCK, PEER_HEADS, PEER_TOPK * PEER_TOPK)
        cand_idx = (i1[..., :, None] * PEER_NKEYS + i2[..., None, :]).reshape(PEER_BLOCK, PEER_HEADS, PEER_TOPK * PEER_TOPK)
        top_s, pos = lax.top_k(cand, PEER_TOPK)
        idx = jnp.take_along_axis(cand_idx, pos, axis=-1)
        g = jax.nn.softmax(top_s, axis=-1).astype(hb.dtype)
        u = jnp.take(expert_u, idx, axis=0)
        act = jax.nn.gelu(jnp.einsum("thkd,td->thk", u, hb))
        vv = jnp.take(expert_v, idx, axis=0)
        return jnp.einsum("thk,thkd->td", g * act, vv)

    out = lax.map(one_block, blocks).reshape(-1, D_MODEL)[:n]
    return out.reshape(*lead, D_MODEL)

def block_forward(x, c, conv_buf, attend, w_ada, b_ada, norm1_gain, norm2_gain, w_in, q_gain, k_gain,
                  conv_w, w_o_att, w_o_conv, w_o, w_pq, sub_keys1, sub_keys2, expert_u, expert_v):
    B, T = x.shape[0], x.shape[1]
    shift1, scale1, gate1, shift2, scale2, gate2 = adaln(c, w_ada, b_ada)
    h = rms_norm(x, norm1_gain) * (1 + scale1) + shift1
    z = h @ w_in
    q, k, v, cb, cc, cx, ga, gb = jnp.split(z, IN_SPLITS, axis=-1)
    q = rms_norm(q.reshape(B, T, ATT_HEADS, HEAD_DIM), q_gain)
    k = rms_norm(k.reshape(B, T, ATT_HEADS, HEAD_DIM), k_gain)
    v = v.reshape(B, T, ATT_HEADS, HEAD_DIM)
    y_att = attend(q, k, v) @ w_o_att
    conv_y, conv_state = causal_short_conv(cc * cx, conv_buf, conv_w)
    y_conv = (cb * conv_y) @ w_o_conv
    mixed = (jax.nn.sigmoid(ga) * y_att + jax.nn.sigmoid(gb) * y_conv) @ w_o
    x = x + gate1 * mixed
    h2 = rms_norm(x, norm2_gain) * (1 + scale2) + shift2
    x = x + gate2 * peer_channel_mixer(h2, w_pq, sub_keys1, sub_keys2, expert_u, expert_v)
    return x, k, v, conv_state

def setup_inputs(seed: int = 0) -> dict:
    key = jax.random.key(seed)
    ks = jax.random.split(key, 28)
    nrm = lambda k, shape, s: jax.random.normal(k, shape, jnp.float32) * s
    att_cache = min(LEFT_CTX, PAST_LEN)
    L = DEPTH
    return {
        "x_prompt": nrm(ks[0], (BATCH, SEQ, D_MODEL), 1.0),
        "c_prompt": nrm(ks[1], (BATCH, D_MODEL), 1.0),
        "x_sample": nrm(ks[2], (DEC_BATCH, DEC_SEQ, D_MODEL), 1.0),
        "c_sample": nrm(ks[3], (DEC_BATCH, D_MODEL), 1.0),
        "cache_k": nrm(ks[4], (L, DEC_BATCH, att_cache, ATT_HEADS, HEAD_DIM), 1.0),
        "cache_v": nrm(ks[5], (L, DEC_BATCH, att_cache, ATT_HEADS, HEAD_DIM), 1.0),
        "cache_conv": nrm(ks[6], (L, DEC_BATCH, CONV_WIDTH - 1, CONV_DIM), 0.5),
        "w_ada": nrm(ks[7], (L, D_MODEL, 6 * D_MODEL), D_MODEL ** -0.5),
        "b_ada": nrm(ks[8], (L, 6 * D_MODEL), 0.02),
        "norm1_gain": 1.0 + nrm(ks[9], (L, D_MODEL), 0.02),
        "norm2_gain": 1.0 + nrm(ks[10], (L, D_MODEL), 0.02),
        "w_in": nrm(ks[11], (L, D_MODEL, IN_COLS), D_MODEL ** -0.5),
        "q_gain": 1.0 + nrm(ks[12], (L, HEAD_DIM), 0.02),
        "k_gain": 1.0 + nrm(ks[13], (L, HEAD_DIM), 0.02),
        "rel_table": nrm(ks[14], (L, ATT_HEADS, N_REL), 0.2),
        "conv_w": nrm(ks[15], (L, CONV_WIDTH, CONV_DIM), CONV_WIDTH ** -0.5),
        "w_o_att": nrm(ks[16], (L, ATT_DIM, D_MODEL), ATT_DIM ** -0.5),
        "w_o_conv": nrm(ks[17], (L, CONV_DIM, D_MODEL), CONV_DIM ** -0.5),
        "w_o": nrm(ks[18], (L, D_MODEL, D_MODEL), D_MODEL ** -0.5),
        "w_pq": nrm(ks[19], (L, D_MODEL, PEER_HEADS * PEER_DKEY), D_MODEL ** -0.5),
        "sub_keys1": nrm(ks[20], (L, PEER_HEADS, PEER_NKEYS, PEER_HALF), PEER_HALF ** -0.5),
        "sub_keys2": nrm(ks[21], (L, PEER_HEADS, PEER_NKEYS, PEER_HALF), PEER_HALF ** -0.5),
        "expert_u": nrm(ks[22], (L, PEER_N, D_MODEL), D_MODEL ** -0.5),
        "expert_v": nrm(ks[23], (L, PEER_N, D_MODEL), 0.5),
    }

def reference(x_prompt, c_prompt, x_sample, c_sample, cache_k, cache_v, cache_conv,
              w_ada, b_ada, norm1_gain, norm2_gain, w_in, q_gain, k_gain, rel_table, conv_w,
              w_o_att, w_o_conv, w_o, w_pq, sub_keys1, sub_keys2, expert_u, expert_v):
    n_keep = min(LEFT_CTX, x_prompt.shape[1])
    xp, xs = x_prompt, x_sample
    kp_l, vp_l, cp_l, ks_l, vs_l, cs_l = [], [], [], [], [], []
    for l in range(DEPTH):
        layer_w = [w[l] for w in (w_ada, b_ada, norm1_gain, norm2_gain, w_in, q_gain, k_gain, conv_w,
                                  w_o_att, w_o_conv, w_o, w_pq, sub_keys1, sub_keys2, expert_u, expert_v)]
        rt = rel_table[l]
        conv_zero = jnp.zeros((xp.shape[0], CONV_WIDTH - 1, CONV_DIM), xp.dtype)
        xp, kp, vp, cp = block_forward(
            xp, c_prompt, conv_zero,
            lambda q, k, v, rt=rt: prompt_band_attention(q, k, v, rt), *layer_w)
        ck, cv = cache_k[l], cache_v[l]
        xs, kn, vn, cn = block_forward(
            xs, c_sample, cache_conv[l],
            lambda q, k, v, rt=rt, ck=ck, cv=cv: sample_band_attention(q, k, v, ck, cv, rt), *layer_w)
        kp_l.append(kp[:, -n_keep:])
        vp_l.append(vp[:, -n_keep:])
        cp_l.append(cp)
        ks_l.append(kn)
        vs_l.append(vn)
        cs_l.append(cn)
    return (xp, xs, jnp.stack(kp_l), jnp.stack(vp_l), jnp.stack(cp_l),
            jnp.stack(ks_l), jnp.stack(vs_l), jnp.stack(cs_l))


_drawn_inputs = setup_inputs


def setup_inputs(seed=0):
    import zlib

    import numpy as np

    out = dict(_drawn_inputs(seed))
    spreads = {}
    factors = {'norm2_gain': 2.929, 'q_gain': 8.0, 'k_gain': 2.799, 'rel_table': 4.088}
    for name, (base, spread) in spreads.items():
        noise = np.random.default_rng([zlib.crc32(name.encode()), seed]).standard_normal(out[name].shape)
        drawn = base * np.exp(spread * noise) if base else spread * noise
        out[name] = __import__('jax').numpy.asarray(drawn.astype(out[name].dtype))
    for name, factor in factors.items():
        out[name] = (out[name] * factor).astype(out[name].dtype)
    return out
```

```python
from contextlib import ExitStack

import concourse.bass as bass
from concourse import mybir

ALU = mybir.AluOpType
ACT = mybir.ActivationFunctionType
AX_X = mybir.AxisListType.X
F32 = mybir.dt.float32
BF16 = mybir.dt.bfloat16
U32 = mybir.dt.uint32
ds = bass.ds

P = 128
D = 1024
KD = D // P
TP = 512
TS = 64
T = TP + TS
HALF = T // 2
NTT = 5
TT = [(128 * i, 128) for i in range(4)] + [(TP, TS)]
GROUP_COLS = [(0, TP), (TP, TS)]
NHEAD = 8
HD = 64
ATT = NHEAD * HD
CONV = 512
CT = CONV // P
PAST = 128
NREL = 257
PH = 8
NKEY = 128
TOPK = 16
NEXP = NKEY * NKEY
EPS = 1e-6
WBLK = 4096
TPAD = NTT * P
GTOK = 32
NGB = T // GTOK
EG = 8

C_BADA, C_G1, C_G2, C_CW, C_CC, C_QG, C_KG, C_C = 0, 48, 56, 64, 76, 84, 85, 86
NVEC = 102
Z_Q, Z_K, Z_V, Z_B, Z_C, Z_X, Z_GA, Z_GC = 0, 4, 8, 12, 16, 20, 24, 32


class Kernel:
    pass


def bc(ap, axis, n):
    wide = ap.unsqueeze(axis)
    shape = list(wide.shape)
    shape[axis] = n
    return wide.to_broadcast(shape)


class Chain:

    def __init__(self, sem, it=0, per=0, start=0):
        self.sem, self.base, self.per, self.n = sem, start + (it * per if per else 0), per, 0

    def did(self, ins):
        ins.then_inc(self.sem, 1)
        self.n += 1
        return self.n

    def at(self, n=None):
        return self.base + (self.n if n is None else n)

    def end(self):
        assert self.n == self.per, (self.n, self.per)


def setup_phase(nc, k, sem):
    s_vec, s_blk, s_const0, s_const, s_vT, s_vTs, s_silu = (sem(n) for n in (
        "vec_loaded", "blk64_set", "const_zeroed", "const_ready", "vec_turned", "vec_ready", "silu_ready"))
    with ExitStack() as ctx:
        vecs = ctx.enter_context(nc.sbuf_tensor("vecs", [P, P], F32))
        psV = ctx.enter_context(nc.psum_tensor("psV", [P, 512], F32))
        with nc.Block() as block:
            @block.sync
            def _(sp):
                loads = [(vecs[C_BADA:C_BADA + 48, :], k.b_ada.rearrange("l (r c) -> (l r) c", c=P)),
                         (vecs[C_G1:C_G1 + 8, :], k.norm1_gain.rearrange("l (r c) -> (l r) c", c=P)),
                         (vecs[C_G2:C_G2 + 8, :], k.norm2_gain.rearrange("l (r c) -> (l r) c", c=P)),
                         (vecs[C_CW:C_CW + 12, :], k.conv_w.rearrange("l w (r c) -> (l w r) c", c=P)),
                         (vecs[C_CC:C_CC + 8, :], k.cache_conv.rearrange("l b w (r c) -> (l b w r) c", c=P)),
                         (vecs[C_QG:C_QG + 1, 0:HD], k.q_gain), (vecs[C_QG:C_QG + 1, HD:P], k.q_gain),
                         (vecs[C_KG:C_KG + 1, 0:HD], k.k_gain), (vecs[C_KG:C_KG + 1, HD:P], k.k_gain),
                         (vecs[C_C:C_C + 8, :], k.c_prompt.rearrange("b (r c) -> (b r) c", c=P)),
                         (vecs[C_C + 8:C_C + 16, :], k.c_sample.rearrange("b (r c) -> (b r) c", c=P))]
                for dst, src in loads:
                    sp.dma_start(dst, src).then_inc(s_vec, 16)
                for i, (t0, w) in enumerate(TT):
                    src = k.x_prompt[0, t0:t0 + w, :] if i < 4 else k.x_sample[0, :, :]
                    sp.dma_start(k.x[0:w, i, :], src).then_inc(k.s_x[i], 16)
                k.n_vec = len(loads)

            @block.gpsimd
            def _(pool):
                nc.gpsimd.memset(k.ident[:, :], 0.0).then_inc(s_const0, 1)
                nc.gpsimd.memset(k.flip[:, :], 0.0).then_inc(s_const0, 1)
                pool.wait_ge(s_const0, 2)
                nc.gpsimd.affine_select(out=k.ident[:, :], in_=k.ident[:, :], compare_op=ALU.not_equal, fill=1.0,
                                        base=0, pattern=[[-1, P]], channel_multiplier=1).then_inc(s_const, 1)
                nc.gpsimd.affine_select(out=k.flip[:, :], in_=k.flip[:, :], compare_op=ALU.not_equal, fill=1.0,
                                        base=-(P - 1), pattern=[[1, P]], channel_multiplier=1).then_inc(s_const, 1)
                pool.wait_ge(s_const, 2)

            @block.tensor
            def _(pe):
                pe.wait_ge(s_vec, 16 * 11)
                pe.wait_ge(s_const, 2)
                nc.tensor.transpose(psV[:, 0:NVEC], vecs[0:NVEC, :], k.ident[0:NVEC, 0:NVEC]).then_inc(s_vT, 1)

            @block.vector
            def _(dve):
                nc.vector.memset(k.blk64[:, :], 0.0).then_inc(s_blk, 1)
                dve.wait_ge(s_blk, 1)
                for a in range(2):
                    nc.vector.memset(k.blk64[a * HD:(a + 1) * HD, a * HD:(a + 1) * HD], 1.0).then_inc(s_blk, 1)
                dve.wait_ge(s_vT, 1)
                nc.vector.tensor_copy(k.vT[:, 0:NVEC], psV[:, 0:NVEC]).then_inc(s_vTs, 1)

            @block.scalar
            def _(act):
                act.wait_ge(s_vTs, 1)
                nc.scalar.activation(k.siluc[:, :, :], k.vT[:, C_C:C_C + 16].rearrange("p (g t) -> p t g", g=2),
                                     ACT.Silu).then_inc(s_silu, 1)
                act.wait_ge(s_silu, 1)


def ada_phase(nc, k, sem):
    s_w = [sem(f"ada_w{i}") for i in range(3)]
    s_mod, s_sq, s_r, s_rc, s_rs, s_xn, s_tp, s_hd, s_ha, s_ab = (sem(n) for n in (
        "mod_ready", "x_squares", "x_mean", "x_inverse", "x_rstd", "xn_ready", "xn_turned", "h_ready_dve", "h_ready_act", "ab_ready"))
    NB = 12
    with ExitStack() as ctx:
        sq = ctx.enter_context(nc.sbuf_tensor("sq", [P, D], F32))
        xn = ctx.enter_context(nc.sbuf_tensor("xn", [P, 2, D], F32))
        st = ctx.enter_context(nc.sbuf_tensor("st", [P, 4, 8], F32))
        psM = ctx.enter_context(nc.psum_tensor("psM", [P, 512], F32))
        psT = ctx.enter_context(nc.psum_tensor("psT", [P, 2, KD, P], F32))
        with nc.Block() as block:
            @block.sync
            def _(sp):
                w_ada = k.w_ada[0].rearrange("(t p) n -> p t n", p=P)
                with sp.Fori(0, NB // 3) as it:
                    for s in range(3):
                        sp.wait_ge(k.s_ring[s], it + 1)
                        sp.dma_start(k.wring[:, s, :].rearrange("p (t n) -> p t n", t=KD),
                                     w_ada[:, :, ds((it * 3 + s) * 512, 512)]).then_inc(s_w[s], 16)

            @block.tensor
            def _(pe):
                for s in range(3):
                    pe.sem_inc(k.s_ring[s], 1)
                with pe.Fori(0, NB // 3) as it:
                    for s in range(3):
                        pe.wait_ge(s_w[s], (it + 1) * 16)
                        if s == 0:
                            pe.wait_ge(s_mod, it + 1)
                        w = k.wring[:, s, :].rearrange("p (t n) -> p t n", t=KD)
                        for c in range(4):
                            j = 4 * s + c
                            for t in range(KD):
                                mm = nc.tensor.matmul(psM[:, 2 * j:2 * j + 2], w[:, t, c * P:(c + 1) * P],
                                                      k.siluc[:, t, :], start=(t == 0), stop=(t == KD - 1))
                        mm.then_inc(k.s_ring[s], 1)
                for i, (t0, w) in enumerate(TT):
                    pe.wait_ge(s_xn, i + 1)
                    if i >= 2:
                        pe.wait_ge(s_hd, KD // 2 * (i - 1))
                        pe.wait_ge(s_ha, KD // 2 * (i - 1))
                    for t in range(KD):
                        mm = nc.tensor.transpose(psT[:, i % 2, t, 0:w], xn[0:w, i % 2, t * P:(t + 1) * P],
                                                 k.ident[0:w, 0:w])
                    mm.then_inc(s_tp, 1)

            @block.vector
            def _(dve):
                dve.sem_inc(s_mod, 1)
                for i, (t0, w) in enumerate(TT):
                    dve.wait_ge(s_sq, i + 1)
                    nc.vector.tensor_scalar(st[0:w, 1, i:i + 1], st[0:w, 0, i:i + 1], 1.0 / D, EPS,
                                            ALU.mult, ALU.add).then_inc(s_r, 1)
                    dve.wait_ge(s_r, i + 1)
                    nc.vector.reciprocal(st[0:w, 2, i:i + 1], st[0:w, 1, i:i + 1]).then_inc(s_rc, 1)
                    if i < 2:
                        dve.wait_ge(s_rs, i + 1)
                        nc.vector.tensor_scalar(xn[0:w, i, :], k.x[0:w, i, :], st[0:w, 3, i:i + 1], None,
                                                ALU.mult).then_inc(s_xn, 1)
                with dve.Fori(0, NB // 3) as it:
                    for s in range(3):
                        dve.wait_ge(k.s_ring[s], it + 2)
                    nc.vector.tensor_tensor(k.mod[:, ds(it * 12, 12), :],
                                            psM[:, 0:24].rearrange("p (j g) -> p j g", g=2),
                                            bc(k.vT[:, ds(it * 12 + C_BADA, 12)], 2, 2), ALU.add).then_inc(s_mod, 1)
                dve.wait_ge(s_mod, 1 + NB // 3)
                for n, cg in ((0, C_G1), (1, C_G2)):
                    nc.vector.tensor_scalar(k.fac[:, n, :, :], k.mod[:, 24 * n + 8:24 * n + 16, :], 1.0, None,
                                            ALU.add).then_inc(s_ab, 1)
                    dve.wait_ge(s_ab, 2 * n + 1)
                    nc.vector.tensor_tensor(k.fac[:, n, :, :], k.fac[:, n, :, :],
                                            bc(k.vT[:, cg:cg + 8], 2, 2), ALU.mult).then_inc(s_ab, 1)
                dve.wait_ge(s_ab, 4)
                for i, (t0, w) in enumerate(TT):
                    g = i // 4
                    dve.wait_ge(s_tp, i + 1)
                    for t in range(0, KD // 2):
                        nc.vector.tensor_scalar(k.hT[:, t, t0:t0 + w], psT[:, i % 2, t, 0:w], k.fac[:, 0, t, g:g + 1],
                                                k.mod[:, t, g:g + 1], ALU.mult, ALU.add).then_inc(s_hd, 1)
                    if i + 2 < NTT:
                        w2 = TT[i + 2][1]
                        dve.wait_ge(s_rs, i + 3)
                        nc.vector.tensor_scalar(xn[0:w2, i % 2, :], k.x[0:w2, i + 2, :], st[0:w2, 3, i + 2:i + 3], None,
                                                ALU.mult).then_inc(s_xn, 1)
            @block.scalar
            def _(act):
                for i, (t0, w) in enumerate(TT):
                    act.wait_ge(k.s_x[i], 16)
                    if i:
                        act.wait_ge(s_sq, i)
                    nc.scalar.activation(sq[0:w, :], k.x[0:w, i, :], ACT.Square,
                                         accum_out=st[0:w, 0, i:i + 1]).then_inc(s_sq, 1)
                for i, (t0, w) in enumerate(TT):
                    act.wait_ge(s_rc, i + 1)
                    nc.scalar.activation(st[0:w, 3, i:i + 1], st[0:w, 2, i:i + 1], ACT.Sqrt).then_inc(s_rs, 1)
                act.wait_ge(s_ab, 4)
                for i, (t0, w) in enumerate(TT):
                    g = i // 4
                    act.wait_ge(s_tp, i + 1)
                    for t in range(KD // 2, KD):
                        nc.scalar.activation(k.hT[:, t, t0:t0 + w], psT[:, i % 2, t, 0:w], ACT.Identity,
                                             bias=k.mod[:, t, g:g + 1], scale=k.fac[:, 0, t, g:g + 1]).then_inc(s_ha, 1)


def z_phase(nc, k, sem):
    s_w = [sem(f"win_w{i}") for i in range(2)]
    s_used = [sem(f"win_used{i}") for i in range(2)]
    s_z, s_za, s_zd = sem("z_tile_done"), sem("z_evicted_act"), sem("z_evicted_dve")
    with ExitStack() as ctx:
        psZ = ctx.enter_context(nc.psum_tensor("psZ", [P, 8, 512], F32))
        with nc.Block() as block:
            @block.sync
            def _(sp):
                w_in = k.w_in[0].rearrange("(t p) n -> p t n", p=P)

                def load(s, col):
                    sp.dma_start(k.wring[:, s, :].rearrange("p (t n) -> p t n", t=KD),
                                 w_in[:, :, ds(col, 512)]).then_inc(s_w[s], 16)
                for s in range(2):
                    load(s, s * 512)
                with sp.Fori(1, 5) as it:
                    for s in range(2):
                        sp.wait_ge(s_used[s], it)
                        load(s, (it * 2 + s) * 512)

            @block.tensor
            def _(pe):
                with pe.Fori(0, 5) as it:
                    for s in range(2):
                        pe.wait_ge(s_w[s], (it + 1) * 16)
                        w = k.wring[:, s, :].rearrange("p (t n) -> p t n", t=KD)
                        for c in range(4):
                            pe.wait_ge(s_za, it * 8 + 4 * s + c + 1)
                            pe.wait_ge(s_zd, it * 8 + 4 * s + c + 1)
                            for t in range(KD):
                                for hf in range(2):
                                    mm = nc.tensor.matmul(psZ[:, 2 * c + hf, 0:HALF], w[:, t, c * P:(c + 1) * P],
                                                          k.hT[:, t, hf * HALF:(hf + 1) * HALF],
                                                          start=(t == 0), stop=(t == KD - 1))
                            mm.then_inc(s_z, 1)
                        pe.wait_ge(s_z, it * 8 + 4 * s + 4)
                        pe.sem_inc(s_used[s], 1)

            def evict(eng, copy, hf, s_out):
                eng.sem_inc(s_out, 4)
                with eng.Fori(0, 10) as it:
                    for c in range(4):
                        eng.wait_ge(s_z, it * 4 + c + 1)
                        copy(k.zT[:, ds(it * 4 + c, 1), hf * HALF:(hf + 1) * HALF],
                             psZ[:, 2 * c + hf:2 * c + hf + 1, 0:HALF]).then_inc(s_out, 1)

            @block.scalar
            def _(act):
                evict(act, nc.scalar.copy, 0, s_za)

            @block.vector
            def _(dve):
                evict(dve, lambda o, i: nc.vector.tensor_scalar(o, i, 1.0, None, ALU.mult), 1, s_zd)


def prep_phase(nc, k, sem):
    s_rel, s_ext, s_extd, s_tt, s_flip, s_bias = (sem(n) for n in (
        "rel_loaded", "rel_extended", "rel_in_dram", "rel_diagonals", "bias_flipped", "bias_ready"))
    s_ck, s_cv, s_kt, s_u, s_cv1, s_st, s_sT, s_so, s_out = (sem(n) for n in (
        "cache_k_loaded", "cache_v_loaded", "cache_k_turned", "conv_input", "conv_step", "conv_state", "conv_state_turned",
        "conv_state_ready", "conv_state_stored"))
    NX = 384
    with ExitStack() as ctx:
        def sb(name, shape):
            return ctx.enter_context(nc.sbuf_tensor(name, shape, F32))
        rel = sb("rel", [NHEAD, NREL])
        ext = sb("ext", [NHEAD, NX])
        diag = sb("diag", [P, NHEAD, 256])
        ck = sb("ck", [P, ATT])
        ubuf = sb("ubuf", [P, CT, T + 4])
        ybuf = sb("ybuf", [P, T + 2])
        cst = sb("cst", [P, 16])
        cso = sb("cso", [16, P])
        psB = ctx.enter_context(nc.psum_tensor("psB", [P, 4, 512], F32))
        psK = ctx.enter_context(nc.psum_tensor("psK", [P, 512], F32))
        psC = ctx.enter_context(nc.psum_tensor("psC", [P, 512], F32))
        with nc.Block() as block:
            @block.sync
            def _(sp):
                sp.dma_start(rel[:, :], k.rel_table[0]).then_inc(s_rel, 16)
                sp.dma_start(ck[:, :], k.cache_k[0, 0].rearrange("t h d -> t (h d)")).then_inc(s_ck, 16)
                sp.dma_start(k.cv[:, :], k.cache_v[0, 0].rearrange("t h d -> t (h d)")).then_inc(s_cv, 16)
                sp.wait_ge(s_ext, 2)
                sp.dma_start(k.rel_ext, ext[:, :]).then_inc(s_extd, 16)
                sp.wait_ge(s_extd, 16)
                src = bass.AP(k.rel_ext.tensor, 0, [[1, P], [NX, NHEAD], [1, 256]])
                sp.dma_start(diag[:, :, :], src).then_inc(s_tt, 16)
                sp.wait_ge(s_so, 1)
                for g, o in enumerate((k.o_conv_p, k.o_conv_s)):
                    sp.dma_start(o.rearrange("l b w (r c) -> (l b w r) c", c=P), cso[8 * g:8 * g + 8, :]).then_inc(s_out, 16)
                sp.wait_ge(s_cv, 16)
                sp.wait_ge(s_out, 32)

            @block.tensor
            def _(pe):
                pe.wait_ge(s_ck, 16)
                for c in range(4):
                    mm = nc.tensor.transpose(psK[:, c * P:(c + 1) * P], ck[:, c * P:(c + 1) * P], k.ident[:, :])
                mm.then_inc(s_kt, 1)
                pe.wait_ge(s_tt, 16)
                for h in range(NHEAD):
                    for o in range(2):
                        mm = nc.tensor.matmul(psB[:, h // 2, (h % 2) * 256 + (1 - o) * P:(h % 2) * 256 + (2 - o) * P],
                                              diag[:, h, o * P:(o + 1) * P], k.flip[:, :], start=True, stop=True)
                mm.then_inc(s_flip, 1)
                pe.wait_ge(s_st, 1)
                nc.tensor.transpose(psC[0:16, 0:P], cst[:, :], k.ident[:, :]).then_inc(s_sT, 1)

            @block.scalar
            def _(act):
                act.wait_ge(s_kt, 1)
                nc.scalar.copy(k.kcT[:, :, :], psK[:, :].rearrange("p (c t) -> p c t", c=4)).then_inc(s_bias, 1)
                act.wait_ge(s_flip, 1)
                for b in range(4):
                    nc.scalar.copy(k.bias[:, 2 * b:2 * b + 2, :], psB[:, b, :].rearrange("p (h m) -> p h m", h=2)).then_inc(s_bias, 1)
                act.wait_ge(s_bias, 5)

            @block.vector
            def _(dve):
                dve.wait_ge(s_rel, 16)
                nc.vector.tensor_copy(ext[:, 0:256], rel[:, 1:257]).then_inc(s_ext, 1)
                nc.vector.tensor_copy(ext[:, 256:NX], rel[:, 256:257].to_broadcast([NHEAD, NX - 256])).then_inc(s_ext, 1)
                nc.vector.memset(ubuf[:, :, 0:2], 0.0).then_inc(s_u, 1)
                nc.vector.tensor_copy(ubuf[:, :, TP + 2:TP + 4],
                                      k.vT[:, C_CC:C_CC + 8].rearrange("p (w c) -> p c w", w=2)).then_inc(s_u, 1)
                for (g0, gw), u0 in zip(GROUP_COLS, (2, TP + 4)):
                    nc.vector.tensor_tensor(ubuf[:, :, u0:u0 + gw], k.zT[:, Z_C:Z_C + CT, g0:g0 + gw],
                                            k.zT[:, Z_X:Z_X + CT, g0:g0 + gw], ALU.mult).then_inc(s_u, 1)
                dve.wait_ge(s_u, 4)
                for g, u0 in enumerate((TP, TP + 2 + TS)):
                    nc.vector.tensor_copy(cst[:, 8 * g:8 * g + 8].rearrange("p (w c) -> p c w", w=2),
                                          ubuf[:, :, u0:u0 + 2]).then_inc(s_u, 1)
                dve.wait_ge(s_u, 6)
                dve.sem_inc(s_st, 1)
                n = Chain(s_cv1)
                for c in range(CT):
                    for w in range(3):
                        wcol = k.vT[:, C_CW + w * CT + c:C_CW + w * CT + c + 1]
                        u = ubuf[:, c, w:w + T + 2]
                        if w == 0:
                            n.did(nc.vector.tensor_scalar(ybuf[:, :], u, wcol, None, ALU.mult))
                        else:
                            n.did(nc.vector.scalar_tensor_tensor(ybuf[:, :], u, wcol, ybuf[:, :], ALU.mult, ALU.add))
                        dve.wait_ge(s_cv1, n.at())
                    for (g0, gw), u0 in zip(GROUP_COLS, (0, TP + 2)):
                        n.did(nc.vector.tensor_tensor(k.zT[:, Z_B + c, g0:g0 + gw], k.zT[:, Z_B + c, g0:g0 + gw],
                                                      ybuf[:, u0:u0 + gw], ALU.mult))
                    dve.wait_ge(s_cv1, n.at())
                dve.wait_ge(s_sT, 1)
                nc.vector.tensor_copy(cso[:, :], psC[0:16, 0:P]).then_inc(s_so, 1)


def attention_phase(nc, k, sem):
    names = ("sq_ready", "sums_ready", "inverse_ready", "root_ready", "normed_ready", "v_staged", "v_turned", "v_ready",
             "k_turned", "k_natural", "kv_stored", "scores_ready", "max_ready", "exp_ready", "probs_ready",
             "probs_turned", "probsT_ready", "out_ready", "out_stored", "dve_step")
    s = {n: sem("att_" + n) for n in names}
    NU = 10
    units = [(i, hh) for i in range(NTT) for hh in range(2)]
    NDVE = 4 + 2 * (3 + 3 + 4 + 4 + 2)
    with ExitStack() as ctx:
        def sb(name, shape):
            return ctx.enter_context(nc.sbuf_tensor(name, shape, F32))
        qk = sb("qk", [P, 2, TPAD])
        nsc = sb("nsc", [P, T])
        vst = sb("vst", [P, T])
        kcs = sb("kcs", [P, P])
        cvs = sb("cvs", [P, P])
        vn = sb("vn", [P, NTT, P])
        kn = sb("kn", [P, NTT, P])
        sc = sb("sc", [P, 2, 512])
        pT = sb("pT", [P, 2, 512])
        stat = sb("stat", [P, 2, 4])
        psN = ctx.enter_context(nc.psum_tensor("psN", [P, 2, 512], F32))
        psS = ctx.enter_context(nc.psum_tensor("psS", [P, 2, 512], F32))
        psP = ctx.enter_context(nc.psum_tensor("psP", [P, 2, 512], F32))
        psO = ctx.enter_context(nc.psum_tensor("psO", [P, 2, 512], F32))

        def keys(i):
            return 128 * (i + 1) if i < 4 else PAST + TS

        def ktiles(i):
            return [(P, j * P) for j in range(i + 1)] if i < 4 else [(P, 0), (TS, P)]

        def done(it, u):
            return it * NU + u + 3

        def freed(it, u):
            return it * NU + u + 1

        with nc.Block() as block:
            @block.sync
            def _(sp):
                sp.sem_inc(s["kv_stored"], 64)
                with sp.Fori(0, 4) as it:
                    col = sp.snap(it * P)
                    for src, ready, op, osm in ((vn, s["v_ready"], k.o_v_p, k.o_v_s), (kn, s["k_natural"], k.o_k_p, k.o_k_s)):
                        sp.wait_ge(ready, it * 2 + 4)
                        sp.dma_start(op[0, 0].rearrange("(i p) h d -> p i (h d)", p=P)[:, :, ds(it * P, P)],
                                     src[:, 0:4, :]).then_inc(s["kv_stored"], 16)
                        sp.dma_start(osm[0, 0].rearrange("t h d -> t (h d)")[:, ds(col, P)],
                                     src[0:TS, 4, :]).then_inc(s["kv_stored"], 16)
                sp.wait_ge(s["kv_stored"], 5 * 64)

            @block.tensor
            def _(pe):
                pe.sem_inc(s["scores_ready"], 2)
                pe.sem_inc(s["probs_turned"], 2)
                pe.sem_inc(s["out_ready"], 2)
                pe.sem_inc(s["k_turned"], 2)

                def scores(it, u):
                    i, hh = units[u]
                    t0, w = TT[i][0], P
                    h0 = hh * HD
                    pe.wait_ge(s["max_ready"], freed(it, u))
                    q = qk[h0:h0 + HD, 0, t0:t0 + w]
                    if i < 4:
                        mm = nc.tensor.matmul(psS[0:w, u % 2, 0:keys(i)], q, qk[h0:h0 + HD, 1, 0:keys(i)],
                                              start=True, stop=True)
                    else:
                        nc.tensor.matmul(psS[0:w, u % 2, 0:PAST], q, kcs[h0:h0 + HD, :], start=True, stop=True)
                        mm = nc.tensor.matmul(psS[0:w, u % 2, PAST:PAST + TS], q, qk[h0:h0 + HD, 1, TP:T],
                                              start=True, stop=True)
                    mm.then_inc(s["scores_ready"], 1)

                def turn(it, u):
                    i, hh = units[u]
                    w = P
                    pe.wait_ge(s["probs_ready"], done(it, u))
                    pe.wait_ge(s["probsT_ready"], freed(it, u))
                    for n, (kw, k0) in enumerate(ktiles(i)):
                        mm = nc.tensor.transpose(psP[0:kw, u % 2, n * P:n * P + w], sc[0:w, u % 2, k0:k0 + kw],
                                                 k.ident[0:w, 0:w])
                    mm.then_inc(s["probs_turned"], 1)

                def values(it, u):
                    i, hh = units[u]
                    w = P
                    pe.wait_ge(s["probsT_ready"], done(it, u))
                    pe.wait_ge(s["out_stored"], freed(it, u))
                    tiles = ktiles(i)
                    for n, (kw, k0) in enumerate(tiles):
                        v = vn[0:kw, n, :] if i < 4 else (cvs[:, :] if n == 0 else vn[0:kw, 4, :])
                        mm = nc.tensor.matmul(psO[:, u % 2, 0:w], v, pT[0:kw, u % 2, n * P:n * P + w],
                                              start=(n == 0), stop=(n == len(tiles) - 1))
                    mm.then_inc(s["out_ready"], 1)

                with pe.Fori(0, 4) as it:
                    for n in range(2):
                        pe.wait_ge(s["sq_ready"], it * 2 + n + 1)
                        if n == 0:
                            pe.wait_ge(s["k_natural"], it * 2 + 2)
                        else:
                            pe.wait_ge(s["dve_step"], it * NDVE + 2)
                        for hf in range(2):
                            mm = nc.tensor.matmul(psN[:, hf, 0:HALF], k.blk64[:, :], nsc[:, hf * HALF:(hf + 1) * HALF],
                                                  start=True, stop=True)
                        mm.then_inc(s["sums_ready"], 1)
                    pe.wait_ge(s["v_staged"], it + 1)
                    pe.wait_ge(s["dve_step"], it * NDVE + 4)
                    for i, (t0, w) in enumerate(TT):
                        mm = nc.tensor.transpose(psN[0:w, i // 4, (i % 4) * P:(i % 4 + 1) * P], vst[:, t0:t0 + w],
                                                 k.ident[:, :])
                    mm.then_inc(s["v_turned"], 1)
                    pe.wait_ge(s["normed_ready"], it * 2 + 3)
                    pe.wait_ge(s["v_ready"], it * 2 + 4)
                    for i, (t0, w) in enumerate(TT):
                        mm = nc.tensor.transpose(psN[0:w, i // 4, (i % 4) * P:(i % 4 + 1) * P], qk[:, 1, t0:t0 + w],
                                                 k.ident[:, :])
                    mm.then_inc(s["k_turned"], 1)
                    scores(it, 0)
                    scores(it, 1)
                    for u in range(NU):
                        turn(it, u)
                        if u:
                            values(it, u - 1)
                        if u + 2 < NU:
                            scores(it, u + 2)
                    values(it, NU - 1)

            @block.scalar
            def _(act):
                act.sem_inc(s["exp_ready"], 2)
                act.sem_inc(s["probsT_ready"], 2)
                act.sem_inc(s["v_ready"], 2)
                act.sem_inc(s["k_natural"], 2)

                def exps(it, u):
                    w, nk = P, keys(units[u][0])
                    act.wait_ge(s["max_ready"], done(it, u))
                    nc.scalar.activation(sc[0:w, u % 2, 0:nk], sc[0:w, u % 2, 0:nk], ACT.Exp,
                                         bias=stat[0:w, u % 2, 0:1], accum_out=stat[0:w, u % 2, 1:2]).then_inc(s["exp_ready"], 1)

                def evict(it, u):
                    i = units[u][0]
                    w = P
                    act.wait_ge(s["probs_turned"], done(it, u))
                    act.wait_ge(s["out_ready"], freed(it, u))
                    if i < 4:
                        nc.scalar.copy(pT[:, u % 2, 0:keys(i)], psP[:, u % 2, 0:keys(i)]).then_inc(s["probsT_ready"], 1)
                    else:
                        nc.scalar.copy(pT[:, u % 2, 0:w], psP[:, u % 2, 0:w])
                        nc.scalar.copy(pT[0:TS, u % 2, P:P + w], psP[0:TS, u % 2, P:P + w]).then_inc(s["probsT_ready"], 1)

                with act.Fori(0, 4) as it:
                    act.wait_ge(s["k_turned"], it + 2)
                    nc.scalar.copy(vst[:, :], k.zT[:, ds(it + Z_V, 1), :]).then_inc(s["v_staged"], 1)
                    act.wait_ge(s["out_ready"], it * NU + 2)
                    nc.scalar.copy(kcs[:, :], k.kcT[:, ds(it, 1), :])
                    nc.scalar.copy(cvs[:, :], k.cv[:, ds(it * P, P)])
                    for n, z0 in enumerate((Z_Q, Z_K)):
                        act.wait_ge(s["normed_ready"], it * 2 + n + 1)
                        nc.scalar.square(nsc[:, :], k.zT[:, ds(it + z0, 1), :]).then_inc(s["sq_ready"], 1)
                        act.wait_ge(s["inverse_ready"], it * 2 + n + 1)
                        nc.scalar.sqrt(nsc[:, :], nsc[:, :]).then_inc(s["root_ready"], 1)
                    for src, dst, ready, turned in ((psN, vn, s["v_ready"], s["v_turned"]), (psN, kn, s["k_natural"], s["k_turned"])):
                        act.wait_ge(turned, it + (1 if dst is vn else 3))
                        if dst is vn:
                            act.wait_ge(s["kv_stored"], it * 64 + 64)
                        nc.scalar.copy(dst[:, 0:4, :], psN[:, 0, :].rearrange("p (i c) -> p i c", i=4)).then_inc(ready, 1)
                        nc.scalar.copy(dst[0:TS, 4, :], psN[0:TS, 1, 0:P]).then_inc(ready, 1)
                    exps(it, 0)
                    exps(it, 1)
                    for u in range(NU):
                        evict(it, u)
                        if u + 2 < NU:
                            exps(it, u + 2)

            @block.vector
            def _(dve):
                dve.sem_inc(s["max_ready"], 2)
                dve.sem_inc(s["probs_ready"], 2)
                dve.sem_inc(s["out_stored"], 2)
                nc.vector.memset(qk[:, :, T:TPAD], 0.0).then_inc(s["normed_ready"], 1)

                def bias_max(n, it, u):
                    i, hh = units[u]
                    w, nk = P, keys(i)
                    dve.wait_ge(s["scores_ready"], done(it, u))
                    dve.wait_ge(s["probs_turned"], freed(it, u))
                    first = nk - 256 if 1 <= i < 4 else 0
                    b = k.bias[0:w, ds(it * 2 + hh, 1), :].rearrange("p a m -> p (a m)")
                    if i == 0:
                        b = b[:, P:2 * P]
                    elif i == 4:
                        b = b[:, 0:nk]
                    if first:
                        n.did(nc.vector.tensor_scalar(sc[0:w, u % 2, 0:first], psS[0:w, u % 2, 0:first], HD ** -0.5,
                                                      b[:, 0:1], ALU.mult, ALU.add))
                    n.did(nc.vector.scalar_tensor_tensor(sc[0:w, u % 2, first:nk], psS[0:w, u % 2, first:nk], HD ** -0.5,
                                                         b, ALU.mult, ALU.add))
                    if i < 4:
                        dve.wait_ge(s["dve_step"], n.at())
                        n.did(nc.vector.memset(sc[0:64, u % 2, nk - 64:nk], -1e30))
                    dve.wait_ge(s["dve_step"], n.at())
                    nc.vector.tensor_reduce(stat[0:w, u % 2, 0:1], sc[0:w, u % 2, 0:nk], AX_X, ALU.max,
                                            negate=True).then_inc(s["max_ready"], 1)

                def normalise(n, it, u):
                    w, nk = P, keys(units[u][0])
                    dve.wait_ge(s["exp_ready"], done(it, u))
                    n.did(nc.vector.reciprocal(stat[0:w, u % 2, 2:3], stat[0:w, u % 2, 1:2]))
                    dve.wait_ge(s["dve_step"], n.at())
                    nc.vector.tensor_scalar(sc[0:w, u % 2, 0:nk], sc[0:w, u % 2, 0:nk], stat[0:w, u % 2, 2:3], None,
                                            ALU.mult).then_inc(s["probs_ready"], 1)

                def store(it, u):
                    i, hh = units[u]
                    t0, w = TT[i]
                    dve.wait_ge(s["out_ready"], done(it, u))
                    nc.vector.tensor_scalar(k.zT[hh * HD:(hh + 1) * HD, ds(it, 1), t0:t0 + w],
                                            psO[hh * HD:(hh + 1) * HD, u % 2:u % 2 + 1, 0:w], 1.0, None,
                                            ALU.mult).then_inc(s["out_stored"], 1)

                with dve.Fori(0, 4) as it:
                    n = Chain(s["dve_step"], it, NDVE)
                    for m, (z0, cg) in enumerate(((Z_Q, C_QG), (Z_K, C_KG))):
                        dve.wait_ge(s["sums_ready"], it * 2 + m + 1)
                        for hf in range(2):
                            n.did(nc.vector.tensor_scalar(nsc[:, hf * HALF:(hf + 1) * HALF], psN[:, hf, 0:HALF], 1.0 / HD,
                                                          EPS, ALU.mult, ALU.add))
                        dve.wait_ge(s["dve_step"], n.at())
                        nc.vector.reciprocal(nsc[:, :], nsc[:, :]).then_inc(s["inverse_ready"], 1)
                        dve.wait_ge(s["root_ready"], it * 2 + m + 1)
                        if m == 0:
                            dve.wait_ge(s["scores_ready"], it * NU + 2)
                            dve.wait_ge(s["k_turned"], it + 2)
                        nc.vector.scalar_tensor_tensor(qk[:, m:m + 1, 0:T], k.zT[:, ds(it + z0, 1), :], k.vT[:, cg:cg + 1],
                                                       nsc[:, :].unsqueeze(1), ALU.mult, ALU.mult).then_inc(s["normed_ready"], 1)
                    bias_max(n, it, 0)
                    bias_max(n, it, 1)
                    for u in range(NU):
                        normalise(n, it, u)
                        if u + 2 < NU:
                            bias_max(n, it, u + 2)
                        if u:
                            store(it, u - 1)
                    store(it, NU - 1)
                    n.end()


def merge_phase(nc, k, sem):
    names = ("sig", "branch", "dve", "merged", "mix", "gated_act", "gated_dve", "turned", "x1")
    s = {n: sem("mg_" + n) for n in names}
    s_w = [sem(f"mg_w{i}") for i in range(4)]
    with ExitStack() as ctx:
        mT = ctx.enter_context(nc.sbuf_tensor("mT", [P, KD, T], F32))
        tmp = ctx.enter_context(nc.sbuf_tensor("tmp", [P, T], F32))
        ps = ctx.enter_context(nc.psum_tensor("psB4", [P, 8, 512], F32))
        gm = k.zT[:, 0:KD, :]

        def halves(ap):
            return ap.rearrange("p (h c) -> p h c", h=2)

        with nc.Block() as block:
            @block.sync
            def _(sp):
                sp.dma_start(k.wring[:, 0, :].rearrange("p (t n) -> p t n", t=4),
                             k.w_o_att[0].rearrange("(t p) n -> p t n", p=P)).then_inc(s_w[0], 16)
                sp.dma_start(k.wring[:, 1, :].rearrange("p (t n) -> p t n", t=4),
                             k.w_o_conv[0].rearrange("(t p) n -> p t n", p=P)).then_inc(s_w[1], 16)
                w_o = k.w_o[0].rearrange("(t p) n -> p t n", p=P)
                sp.dma_start(k.wring[:, 2, :].rearrange("p (t n) -> p t n", t=KD), w_o[:, :, 0:512]).then_inc(s_w[2], 16)
                sp.wait_ge(s["branch"], KD)
                sp.dma_start(k.wring[:, 0, :].rearrange("p (t n) -> p t n", t=KD), w_o[:, :, 512:D]).then_inc(s_w[3], 16)

            @block.tensor
            def _(pe):
                pe.wait_ge(s_w[0], 16)
                pe.wait_ge(s_w[1], 16)
                for d in range(KD):
                    if d >= 2:
                        pe.wait_ge(s["dve"], 2 * (d - 1))
                    for br, z0 in ((0, 0), (1, Z_B)):
                        w = k.wring[:, br, :].rearrange("p (t n) -> p t n", t=4)
                        for t in range(4):
                            for hf in range(2):
                                mm = nc.tensor.matmul(ps[:, 4 * (d % 2) + 2 * br + hf, 0:HALF], w[:, t, d * P:(d + 1) * P],
                                                      k.zT[:, z0 + t, hf * HALF:(hf + 1) * HALF],
                                                      start=(t == 0), stop=(t == 3))
                    mm.then_inc(s["branch"], 1)
                pe.wait_ge(s["merged"], KD)
                for d in range(KD):
                    if d == 0:
                        pe.wait_ge(s_w[2], 16)
                    if d == 4:
                        pe.wait_ge(s_w[3], 16)
                    if d >= 4:
                        pe.wait_ge(s["gated_act"], d - 3)
                        pe.wait_ge(s["gated_dve"], 2 * (d - 3))
                    w = k.wring[:, 2 if d < 4 else 0, :].rearrange("p (t n) -> p t n", t=KD)
                    for t in range(KD):
                        for hf in range(2):
                            mm = nc.tensor.matmul(ps[:, 2 * (d % 4) + hf, 0:HALF], w[:, t, (d % 4) * P:(d % 4 + 1) * P],
                                                  mT[:, t, hf * HALF:(hf + 1) * HALF], start=(t == 0), stop=(t == KD - 1))
                    mm.then_inc(s["mix"], 1)
                pe.wait_ge(s["gated_act"], KD)
                pe.wait_ge(s["gated_dve"], 2 * KD)
                for i, (t0, w) in enumerate(TT):
                    if i == 4:
                        pe.wait_ge(s["x1"], 1)
                    for d in range(KD):
                        mm = nc.tensor.transpose(ps[0:w, 2 * (i % 4) + d // 4, (d % 4) * P:(d % 4 + 1) * P],
                                                 gm[:, d, t0:t0 + w], k.ident[:, :])
                    mm.then_inc(s["turned"], 1)

            @block.scalar
            def _(act):
                for d in range(KD):
                    for z0 in (Z_GA, Z_GC):
                        nc.scalar.activation(k.zT[:, z0 + d, :], k.zT[:, z0 + d, :], ACT.Sigmoid).then_inc(s["sig"], 1)
                for d in range(KD):
                    act.wait_ge(s["mix"], d + 1)
                    nc.scalar.mul(gm[:, d, 0:HALF], ps[:, 2 * (d % 4), 0:HALF], k.mod[:, 16 + d, 0:1]).then_inc(s["gated_act"], 1)

            @block.vector
            def _(dve):
                for d in range(KD):
                    dve.wait_ge(s["branch"], d + 1)
                    dve.wait_ge(s["sig"], 2 * (d + 1))
                    b = 4 * (d % 2)
                    nc.vector.tensor_tensor(halves(mT[:, d, :]), ps[:, b:b + 2, 0:HALF], halves(k.zT[:, Z_GA + d, :]),
                                            ALU.mult).then_inc(s["dve"], 1)
                    if d:
                        dve.wait_ge(s["merged"], d)
                    nc.vector.tensor_tensor(halves(tmp[:, :]), ps[:, b + 2:b + 4, 0:HALF], halves(k.zT[:, Z_GC + d, :]),
                                            ALU.mult).then_inc(s["dve"], 1)
                    dve.wait_ge(s["dve"], 2 * (d + 1))
                    nc.vector.tensor_tensor(mT[:, d, :], mT[:, d, :], tmp[:, :], ALU.add).then_inc(s["merged"], 1)
                for d in range(KD):
                    dve.wait_ge(s["mix"], d + 1)
                    for g, (a, b) in enumerate(((HALF, TP), (TP, T))):
                        nc.vector.tensor_scalar(gm[:, d, a:b], ps[:, 2 * (d % 4) + 1, a - HALF:b - HALF],
                                                k.mod[:, 16 + d, g:g + 1], None, ALU.mult).then_inc(s["gated_dve"], 1)
                for i, (t0, w) in enumerate(TT):
                    dve.wait_ge(s["turned"], i + 1)
                    b = 2 * (i % 4)
                    xv = k.x[0:w, i, :].rearrange("p (h c) -> p h c", h=2)
                    nc.vector.tensor_tensor(xv, xv, ps[0:w, b:b + 2, :], ALU.add).then_inc(s["x1"], 1)


def norm2_phase(nc, k, sem):
    names = ("sq", "mean", "inv", "root", "xn", "turned", "h_dve", "h_act", "hi", "lo", "zero")
    s = {n: sem("n2_" + n) for n in names}
    with ExitStack() as ctx:
        sq = ctx.enter_context(nc.sbuf_tensor("sq2", [P, D], F32))
        xn = ctx.enter_context(nc.sbuf_tensor("xn2", [P, 2, D], F32))
        st = ctx.enter_context(nc.sbuf_tensor("st2", [P, 4, 8], F32))
        psT = ctx.enter_context(nc.psum_tensor("psT2", [P, 2, KD, P], F32))
        with nc.Block() as block:
            @block.sync
            def _(sp):
                sp.dma_start(k.wpq[:, :, :], k.w_pq[0].rearrange("(t p) n -> p t n", p=P)).then_inc(k.s_wpq, 16)
                for n, src in enumerate((k.sub_keys1, k.sub_keys2)):
                    sp.dma_start(k.subk[:, :, n, :], src[0].rearrange("h q d -> q h d")).then_inc(k.s_subk, 16)

            @block.tensor
            def _(pe):
                for i, (t0, w) in enumerate(TT):
                    pe.wait_ge(s["xn"], i + 1)
                    if i >= 2:
                        pe.wait_ge(s["h_dve"], 4 * (i - 1))
                        pe.wait_ge(s["h_act"], 4 * (i - 1))
                    for t in range(KD):
                        mm = nc.tensor.transpose(psT[:, i % 2, t, 0:w], xn[0:w, i % 2, t * P:(t + 1) * P],
                                                 k.ident[0:w, 0:w])
                    mm.then_inc(s["turned"], 1)

            @block.scalar
            def _(act):
                for i, (t0, w) in enumerate(TT):
                    if i:
                        act.wait_ge(s["sq"], i)
                    nc.scalar.activation(sq[0:w, :], k.x[0:w, i, :], ACT.Square,
                                         accum_out=st[0:w, 0, i:i + 1]).then_inc(s["sq"], 1)
                for i, (t0, w) in enumerate(TT):
                    act.wait_ge(s["inv"], i + 1)
                    nc.scalar.activation(st[0:w, 3, i:i + 1], st[0:w, 2, i:i + 1], ACT.Sqrt).then_inc(s["root"], 1)
                for i, (t0, w) in enumerate(TT):
                    g = i // 4
                    act.wait_ge(s["turned"], i + 1)
                    for t in range(KD // 2, KD):
                        nc.scalar.activation(k.h2T[:, t, t0:t0 + w], psT[:, i % 2, t, 0:w], ACT.Identity,
                                             bias=k.mod[:, 24 + t, g:g + 1], scale=k.fac[:, 1, t, g:g + 1]).then_inc(s["h_act"], 1)
                    act.wait_ge(s["h_dve"], 4 * (i + 1))
                    act.wait_ge(s["h_act"], 4 * (i + 1))
                    nc.scalar.copy(k.h2hi[:, :, t0:t0 + w], k.h2T[:, :, t0:t0 + w]).then_inc(s["hi"], 1)

            @block.vector
            def _(dve):
                nc.vector.memset(k.h2T[:, :, T:TPAD], 0.0).then_inc(s["zero"], 1)
                for i, (t0, w) in enumerate(TT):
                    dve.wait_ge(s["sq"], i + 1)
                    nc.vector.tensor_scalar(st[0:w, 1, i:i + 1], st[0:w, 0, i:i + 1], 1.0 / D, EPS,
                                            ALU.mult, ALU.add).then_inc(s["mean"], 1)
                    dve.wait_ge(s["mean"], i + 1)
                    nc.vector.reciprocal(st[0:w, 2, i:i + 1], st[0:w, 1, i:i + 1]).then_inc(s["inv"], 1)

                def scale(i):
                    w = TT[i][1]
                    dve.wait_ge(s["root"], i + 1)
                    nc.vector.tensor_scalar(xn[0:w, i % 2, :], k.x[0:w, i, :], st[0:w, 3, i:i + 1], None,
                                            ALU.mult).then_inc(s["xn"], 1)
                scale(0)
                scale(1)
                for i, (t0, w) in enumerate(TT):
                    g = i // 4
                    dve.wait_ge(s["turned"], i + 1)
                    if i + 2 < NTT:
                        scale(i + 2)
                    for t in range(KD // 2):
                        nc.vector.tensor_scalar(k.h2T[:, t, t0:t0 + w], psT[:, i % 2, t, 0:w], k.fac[:, 1, t, g:g + 1],
                                                k.mod[:, 24 + t, g:g + 1], ALU.mult, ALU.add).then_inc(s["h_dve"], 1)
                    dve.wait_ge(s["hi"], i + 1)
                    nc.vector.tensor_tensor(k.h2lo[:, :, t0:t0 + w], k.h2T[:, :, t0:t0 + w], k.h2hi[:, :, t0:t0 + w],
                                            ALU.subtract).then_inc(s["lo"], 1)


def topk_phase(nc, k, sem):
    names = ("keys", "keysT", "q_ps", "q_sb", "s_ps", "s_sb", "best", "dve", "shifted", "exp", "rows", "turned",
             "stored", "iota")
    s = {n: sem("tk_" + n) for n in names}
    M = 2 * PH
    NK = PH * TOPK
    NDVE = 5 * M + 2 + 5 * PH + 4 + 6 + 2 + 5
    with ExitStack() as ctx:
        def sb(name, shape, dt=F32):
            return ctx.enter_context(nc.sbuf_tensor(name, shape, dt))
        skT = sb("skT", [P, M, NKEY])
        qT = sb("qT", [P, M, P])
        sc = sb("sc2", [P, M, NKEY])
        left = sb("left", [P, M, NKEY])
        cand = sb("cand", [P, PH, TOPK * TOPK])
        eq = left[:, :, :].rearrange("p m c -> p (m c)").rearrange("p (n a) -> p n a", a=TOPK)
        val = sb("val", [P, M, TOPK])
        idx = sb("idx", [P, M, TOPK], U32)
        idxf = sb("idxf", [P, M, TOPK])
        top = sb("top", [P, PH, TOPK])
        pos = sb("pos", [P, PH, TOPK], U32)
        posu = sb("posu", [P, 2, PH, TOPK], U32)
        posf = sb("posf", [P, 2, PH, TOPK])
        rows = sb("rows", [P, 3, NK])
        esum = sb("esum", [P, 2, PH])
        ghi = sb("ghi", [P, P], BF16)
        carrier = sb("carrier", [P, 1])
        iota16 = sb("iota16", [P, TOPK])
        psQ = ctx.enter_context(nc.psum_tensor("psQ", [P, 2, 512], F32))
        psS = ctx.enter_context(nc.psum_tensor("psS2", [P, 2, 512], F32))
        psX = ctx.enter_context(nc.psum_tensor("psX", [P, 512], F32))
        with nc.Block() as block:
            @block.gpsimd
            def _(pool):
                nc.gpsimd.iota(iota16[:, :], [[1, TOPK]], base=0, channel_multiplier=0,
                               allow_small_or_imprecise_dtypes=True).then_inc(s["iota"], 1)
                pool.wait_ge(s["iota"], 1)
                nc.gpsimd.iota(k.iota128[:, :], [[1, P]], base=0, channel_multiplier=0,
                               allow_small_or_imprecise_dtypes=True).then_inc(s["iota"], 1)

            @block.tensor
            def _(pe):
                pe.wait_ge(k.s_subk, 32)
                for j in range(4):
                    if j >= 2:
                        pe.wait_ge(s["keysT"], j - 1)
                    for c in range(4):
                        m = 4 * j + c
                        mm = nc.tensor.transpose(psQ[:, j % 2, c * P:(c + 1) * P], k.subk[:, m // 2, m % 2, :], k.ident[:, :])
                    mm.then_inc(s["keys"], 1)
                pe.wait_ge(s["keysT"], 4)
                pe.wait_ge(k.s_wpq, 16)
                with pe.Fori(0, NTT) as it:
                    def queries(j):
                        pe.wait_ge(s["q_sb"], it * 4 + j + 1)
                        for c in range(4):
                            m = 4 * j + c
                            for t in range(KD):
                                mm = nc.tensor.matmul(psQ[:, j % 2, c * P:(c + 1) * P], k.wpq[:, t, m * P:(m + 1) * P],
                                                      k.h2T[:, t, ds(it * P, P)], start=(t == 0), stop=(t == KD - 1))
                        mm.then_inc(s["q_ps"], 1)

                    def scores(j):
                        pe.wait_ge(s["q_sb"], it * 4 + j + 3)
                        pe.wait_ge(s["s_sb"], it * 4 + j + 1)
                        for c in range(4):
                            m = 4 * j + c
                            mm = nc.tensor.matmul(psS[:, j % 2, c * P:(c + 1) * P], qT[:, m, :], skT[:, m, :],
                                                  start=True, stop=True)
                        mm.then_inc(s["s_ps"], 1)
                    queries(0)
                    for j in range(4):
                        if j < 3:
                            queries(j + 1)
                        scores(j)
                    pe.wait_ge(s["rows"], it + 1)
                    for n in range(3):
                        mm = nc.tensor.transpose(psX[:, n * P:(n + 1) * P], rows[:, n, :], k.ident[:, :])
                    mm.then_inc(s["turned"], 1)

            @block.scalar
            def _(act):
                act.sem_inc(s["q_sb"], 2)
                act.sem_inc(s["s_sb"], 2)
                for j in range(4):
                    act.wait_ge(s["keys"], j + 1)
                    nc.scalar.copy(skT[:, 4 * j:4 * j + 4, :], psQ[:, j % 2, :].rearrange("p (c q) -> p c q", c=4)).then_inc(s["keysT"], 1)
                with act.Fori(0, NTT) as it:
                    for j in range(4):
                        act.wait_ge(s["q_ps"], it * 4 + j + 1)
                        nc.scalar.copy(qT[:, 4 * j:4 * j + 4, :], psQ[:, j % 2, :].rearrange("p (c q) -> p c q", c=4)).then_inc(s["q_sb"], 1)
                        act.wait_ge(s["s_ps"], it * 4 + j + 1)
                        if j == 0:
                            act.wait_ge(s["best"], it + 1)
                        nc.scalar.copy(sc[:, 4 * j:4 * j + 4, :], psS[:, j % 2, :].rearrange("p (c q) -> p c q", c=4)).then_inc(s["s_sb"], 1)
                    act.wait_ge(s["shifted"], it + 1)
                    nc.scalar.activation(top[:, :, :], top[:, :, :], ACT.Exp).then_inc(s["exp"], 1)

            @block.vector
            def _(dve):
                dve.sem_inc(s["best"], 1)
                dve.wait_ge(s["iota"], 2)
                with dve.Fori(0, NTT) as it:
                    n = Chain(s["dve"], it, NDVE)

                    def settle():
                        dve.wait_ge(s["dve"], n.at())

                    def stand():
                        nc.vector.memset(carrier[:, :], 0.0)

                    def best16(src, rest, v, ix, count):
                        for m in range(count):
                            n.did(nc.vector.max(v[:, m, 0:8], src[:, m, :]))
                        settle()
                        stand()
                        for m in range(count):
                            n.did(nc.vector.max_index(ix[:, m, 0:8], v[:, m, 0:8], src[:, m, :]))
                            n.did(nc.vector.match_replace(rest[:, m, :], v[:, m, 0:8], src[:, m, :], -3.0e38))
                        settle()
                        stand()
                        for m in range(count):
                            n.did(nc.vector.max(v[:, m, 8:16], rest[:, m, :]))
                        settle()
                        stand()
                        for m in range(count):
                            n.did(nc.vector.max_index(ix[:, m, 8:16], v[:, m, 8:16], rest[:, m, :]))
                        settle()
                    dve.wait_ge(s["s_sb"], it * 4 + 6)
                    stand()
                    best16(sc, left, val, idx, M)
                    dve.sem_inc(s["best"], 1)
                    n.did(nc.vector.tensor_copy(idxf[:, :, :], idx[:, :, :]))
                    v = val[:, :, :].rearrange("p (h n) a -> p h n a", n=2)
                    n.did(nc.vector.tensor_tensor(cand[:, :, :].rearrange("p h (a b) -> p h a b", a=TOPK),
                                                  bc(v[:, :, 0, :], 3, TOPK), bc(v[:, :, 1, :], 2, TOPK), ALU.add))
                    settle()
                    stand()
                    cleft = left[:, :, :].rearrange("p (h n) c -> p h (n c)", n=2)
                    best16(cand, cleft, top, pos, PH)
                    n.did(nc.vector.tensor_scalar(posu[:, 0, :, :], pos[:, :, :], 4, None, ALU.logical_shift_right))
                    n.did(nc.vector.tensor_scalar(posu[:, 1, :, :], pos[:, :, :], 15, None, ALU.bitwise_and))
                    n.did(nc.vector.tensor_copy(esum[:, 0, :], top[:, :, 0]))
                    settle()
                    n.did(nc.vector.tensor_copy(posf[:, :, :, :], posu[:, :, :, :]))
                    nc.vector.tensor_tensor(top[:, :, :], top[:, :, :], bc(esum[:, 0, :], 2, TOPK), ALU.subtract).then_inc(s["shifted"], 1)
                    settle()
                    fi = idxf[:, :, :].rearrange("p (h n) a -> p h n a", n=2)
                    e4 = eq.rearrange("p (h k) a -> p h k a", h=PH)
                    for side in range(2):
                        n.did(nc.vector.tensor_tensor(eq, bc(posf[:, side, :, :].rearrange("p h k -> p (h k)"), 2, TOPK),
                                                      bc(iota16[:, :], 1, NK), ALU.is_equal))
                        settle()
                        n.did(nc.vector.tensor_tensor(e4, e4, bc(fi[:, :, side, :], 2, TOPK), ALU.mult))
                        settle()
                        n.did(nc.vector.tensor_reduce(rows[:, side, :], eq, AX_X, ALU.add))
                        settle()
                    dve.wait_ge(s["exp"], it + 1)
                    n.did(nc.vector.tensor_reduce(esum[:, 0, :], top[:, :, :], AX_X, ALU.add))
                    settle()
                    n.did(nc.vector.reciprocal(esum[:, 1, :], esum[:, 0, :]))
                    settle()
                    nc.vector.tensor_tensor(rows[:, 2, :].rearrange("p (h k) -> p h k", h=PH), top[:, :, :],
                                            bc(esum[:, 1, :], 2, TOPK), ALU.mult).then_inc(s["rows"], 1)
                    dve.wait_ge(s["turned"], it + 1)
                    n.did(nc.vector.tensor_copy(ghi[:, :], psX[:, 2 * P:3 * P]))
                    for f in range(2):
                        n.did(nc.vector.tensor_scalar(k.pairs[:, f:f + 1, ds(it * P, P)], psX[:, f * P:(f + 1) * P].unsqueeze(1),
                                                      1.0, None, ALU.mult))
                    settle()
                    n.did(nc.vector.tensor_scalar(k.pairs[:, 2:3, ds(it * P, P)], ghi[:, :].unsqueeze(1), 1.0, None, ALU.mult))
                    n.did(nc.vector.tensor_tensor(k.pairs[:, 3:4, ds(it * P, P)], psX[:, 2 * P:3 * P].unsqueeze(1),
                                                  ghi[:, :].unsqueeze(1), ALU.subtract))
                    settle()
                    n.end()


def gates_phase(nc, k, sem):
    names = ("staged", "hot", "made", "evicted", "stage_used")
    s = {n: sem("gt_" + n) for n in names}
    s_out = [sem(f"gt_out{i}") for i in range(2)]
    NG = GTOK // 4
    with ExitStack() as ctx:
        stg = ctx.enter_context(nc.sbuf_tensor("stg", [P, 2, 4, GTOK], F32))
        hot = ctx.enter_context(nc.sbuf_tensor("hot", [P, 2, 4, 3, P], BF16))
        gst = ctx.enter_context(nc.sbuf_tensor("gst", [P, 2, P, GTOK], F32))
        psG = ctx.enter_context(nc.psum_tensor("psG", [P, 2, 512], F32))
        with nc.Block() as block:
            @block.vector
            def _(dve):
                dve.sem_inc(s["hot"], 2)
                with dve.Fori(0, NGB // 2) as it:
                    for b in range(2):
                        nc.vector.tensor_scalar(stg[:, b, :, :], k.pairs[:, :, ds(it * 2 * GTOK + b * GTOK, GTOK)], 1.0, None,
                                                ALU.mult).then_inc(s["staged"], 1)
                        dve.wait_ge(s["staged"], it * 2 + b + 1)
                        for g in range(NG):
                            u = b * NG + g
                            dve.wait_ge(s["made"], it * 2 * NG + u + 1)
                            for c in range(4):
                                t = 4 * g + c
                                col = [stg[:, b, f, t:t + 1] for f in range(4)]
                                nc.vector.tensor_scalar(hot[:, g % 2, c, 0, :], k.iota128[:, :], col[0], None, ALU.is_equal)
                                for f in range(2):
                                    ins = nc.vector.tensor_scalar(hot[:, g % 2, c, 1 + f, :], k.iota128[:, :], col[1],
                                                                  col[2 + f], ALU.is_equal, ALU.mult)
                            ins.then_inc(s["hot"], 1)

            @block.tensor
            def _(pe):
                pe.sem_inc(s["made"], 2)
                with pe.Fori(0, NGB // 2) as it:
                    for u in range(2 * NG):
                        pe.wait_ge(s["hot"], it * 2 * NG + u + 3)
                        pe.wait_ge(s["evicted"], it * 2 * NG + u + 1)
                        for c in range(4):
                            for f in range(2):
                                mm = nc.tensor.matmul(psG[:, u % 2, c * P:(c + 1) * P], hot[:, u % 2, c, 1 + f, :],
                                                      hot[:, u % 2, c, 0, :], start=(f == 0), stop=(f == 1))
                        mm.then_inc(s["made"], 1)

            @block.scalar
            def _(act):
                act.sem_inc(s["evicted"], 2)
                for b in range(2):
                    act.sem_inc(s_out[b], 16)
                with act.Fori(0, NGB // 2) as it:
                    for b in range(2):
                        act.wait_ge(s_out[b], it * 16 + 16)
                        for g in range(NG):
                            u = b * NG + g
                            act.wait_ge(s["made"], it * 2 * NG + u + 3)
                            nc.scalar.copy(gst[:, b, :, 4 * g:4 * g + 4].rearrange("p i t -> p t i"),
                                           psG[:, u % 2, :].rearrange("p (t i) -> p t i", t=4)).then_inc(s["evicted"], 1)
                        act.wait_ge(s["evicted"], it * 2 * NG + b * NG + NG + 2)
                        act.dma_start(k.gate_dram[ds(it * 2 + b, 1)].rearrange("b p i t -> p b (i t)"),
                                      gst[:, b:b + 1, :, :].rearrange("p b i t -> p b (i t)")).then_inc(s_out[b], 16)
                for b in range(2):
                    act.wait_ge(s_out[b], 16 * (NGB // 2 + 1))


def up_phase(nc, k, sem):
    names = ("turned", "hi", "lo", "up", "gelu")
    s = {n: sem("up_" + n) for n in names}
    s_u = [sem(f"up_u{i}") for i in range(4)]
    s_a = [sem(f"up_a{i}") for i in range(2)]
    NE = NEXP // P
    R = 4
    with ExitStack() as ctx:
        uraw = ctx.enter_context(nc.sbuf_tensor("uraw", [P, R, D], F32))
        uhi = ctx.enter_context(nc.sbuf_tensor("uhi", [P, 2, KD, P], BF16))
        ulo = ctx.enter_context(nc.sbuf_tensor("ulo", [P, 2, KD, P], BF16))
        aout = ctx.enter_context(nc.sbuf_tensor("aout", [P, 2, T], F32))
        psT = ctx.enter_context(nc.psum_tensor("psT3", [P, 2, KD, P], F32))
        psD = ctx.enter_context(nc.psum_tensor("psD", [P, 2, 2, 512], F32))

        with nc.Block() as block:
            @block.sync
            def _(sp):
                def load(it, r):
                    sp.dma_start(uraw[:, r:r + 1, :], k.expert_u[0].rearrange("(e p) d -> p e d", p=P)
                                 [:, ds(it * R + r, 1), :]).then_inc(s_u[r], 16)
                for r in range(R):
                    load(0, r)
                with sp.Fori(1, NE // R) as it:
                    for r in range(R):
                        sp.wait_ge(s["turned"], it * R + r - R + 1)
                        load(it, r)

            @block.tensor
            def _(pe):
                pe.sem_inc(s["up"], 2)

                def turn(it, r):
                    e = it * R + r
                    pe.wait_ge(s_u[r % R], (it + r // R) * 16 + 16)
                    pe.wait_ge(s["lo"], e + 1)
                    for t in range(KD):
                        mm = nc.tensor.transpose(psT[:, r % 2, t, :], uraw[:, r % R, t * P:(t + 1) * P], k.ident[:, :])
                    mm.then_inc(s["turned"], 1)

                def up(it, r):
                    e = it * R + r
                    pe.wait_ge(s["lo"], e + 3)
                    pe.wait_ge(s["gelu"], e + 1)
                    q = r % 2
                    for t in range(KD):
                        for w, hs in ((uhi, (k.h2hi, k.h2lo)), (ulo, (k.h2hi,))):
                            for n, hx in enumerate(hs):
                                for hf in range(2):
                                    mm = nc.tensor.matmul(psD[:, q, hf, 0:HALF], w[:, q, t, :],
                                                          hx[:, t, hf * HALF:(hf + 1) * HALF],
                                                          start=(t == 0 and w is uhi and n == 0),
                                                          stop=(t == KD - 1 and w is ulo))
                    mm.then_inc(s["up"], 1)

                turn(0, 0)
                with pe.Fori(0, NE // R - 1) as it:
                    for r in range(R):
                        turn(it, r + 1)
                        up(it, r)
                for r in range(R):
                    if r < R - 1:
                        turn(NE // R - 1, r + 1)
                    up(NE // R - 1, r)

            @block.scalar
            def _(act):
                act.sem_inc(s["gelu"], 2)
                for q in range(2):
                    act.sem_inc(s_a[q], 16)

                def high(it, r):
                    e = it * R + r
                    act.wait_ge(s["turned"], e + 1)
                    act.wait_ge(s["up"], e + 1)
                    nc.scalar.copy(uhi[:, r % 2, :, :], psT[:, r % 2, :, :]).then_inc(s["hi"], 1)

                def gelu(it, r):
                    e = it * R + r
                    act.wait_ge(s["up"], e + 3)
                    act.wait_ge(s_a[r % 2], (2 * it + r // 2 + 1) * 16)
                    nc.scalar.activation(aout[:, r % 2, :].rearrange("p (h c) -> p h c", h=2), psD[:, r % 2, :, 0:HALF],
                                         ACT.Gelu_apprx_tanh).then_inc(s["gelu"], 1)
                    act.wait_ge(s["gelu"], e + 3)
                    act.dma_start(k.act_dram[ds(it * R + r, 1)].rearrange("e p t -> p e t"),
                                  aout[:, r % 2:r % 2 + 1, :]).then_inc(s_a[r % 2], 16)

                high(0, 0)
                with act.Fori(0, NE // R - 1) as it:
                    for r in range(R):
                        high(it, r + 1)
                        gelu(it, r)
                for r in range(R):
                    if r < R - 1:
                        high(NE // R - 1, r + 1)
                    gelu(NE // R - 1, r)
                for q in range(2):
                    act.wait_ge(s_a[q], 16 * (NE // 2 + 1))

            @block.vector
            def _(dve):
                dve.sem_inc(s["lo"], 2)
                with dve.Fori(0, NE // R) as it:
                    for r in range(R):
                        dve.wait_ge(s["hi"], it * R + r + 1)
                        nc.vector.tensor_tensor(ulo[:, r % 2, :, :], psT[:, r % 2, :, :], uhi[:, r % 2, :, :],
                                                ALU.subtract).then_inc(s["lo"], 1)


def down_phase(nc, k, sem):
    names = ("v_hi", "v_lo", "w", "w_hi", "w_lo", "down", "sum", "zero")
    s = {n: sem("dn_" + n) for n in names}
    s_v = [sem(f"dn_v{i}") for i in range(4)]
    s_a = [sem(f"dn_a{i}") for i in range(4)]
    s_g = [sem(f"dn_g{i}") for i in range(2)]
    NGR = NEXP // P // EG
    with ExitStack() as ctx:
        def sb(name, shape, dt=F32):
            return ctx.enter_context(nc.sbuf_tensor(name, shape, dt))
        vraw = sb("vraw", [P, 4, D])
        abuf = sb("abuf", [P, 4, T])
        gbuf = sb("gbuf", [P, 2, NGB, 4 * GTOK])
        wf = sb("wf", [P, 2, T])
        vh = sb("vh", [P, 2, EG, D], BF16)
        vl = sb("vl", [P, 2, EG, D], BF16)
        wh = sb("wh", [P, 2, EG, T], BF16)
        wl = sb("wl", [P, 2, EG, T], BF16)
        psY = ctx.enter_context(nc.psum_tensor("psY", [P, 4, 2, 512], F32))

        with nc.Block() as block:
            @block.sync
            def _(sp):
                def load(it, b, e, first=False):
                    n = it * 2 * EG + b * EG + e
                    if e % 4 == 0:
                        hf = e // 4
                        if not first:
                            sp.wait_ge(s["w"], n - 4)
                        sp.dma_start(gbuf[:, hf, :, :], k.gate_dram.rearrange("b p i t -> p b (i t)")
                                     [:, :, ds(n * GTOK, 4 * GTOK)]).then_inc(s_g[hf], 16)
                    if not (first and e < 4):
                        sp.wait_ge(s["w"], n - 3)
                    sp.dma_start(abuf[:, e % 4:e % 4 + 1, :], k.act_dram.rearrange("e p t -> p e t")
                                 [:, ds(n, 1), :]).then_inc(s_a[e % 4], 16)
                    if not (first and e < 4):
                        sp.wait_ge(s["v_lo"], n - 3)
                    sp.dma_start(vraw[:, e % 4:e % 4 + 1, :], k.expert_v[0].rearrange("(e p) d -> p e d", p=P)
                                 [:, ds(n, 1), :]).then_inc(s_v[e % 4], 16)
                for e in range(EG):
                    load(0, 0, e, True)
                for e in range(EG):
                    load(0, 1, e)
                with sp.Fori(1, NGR // 2) as it:
                    for b in range(2):
                        for e in range(EG):
                            load(it, b, e)

            @block.scalar
            def _(act):
                def split(it, b, e):
                    n = it * 2 * EG + b * EG + e
                    act.wait_ge(s_v[e % 4], (it * 4 + b * 2 + e // 4 + 1) * 16)
                    if e == 0:
                        act.wait_ge(s["down"], it * 2 * KD + b * KD + 1)
                    nc.scalar.copy(vh[:, b, e, :], vraw[:, e % 4, :]).then_inc(s["v_hi"], 1)
                    act.wait_ge(s["w"], n + 1)
                    nc.scalar.copy(wh[:, b, e, :], wf[:, e % 2, :]).then_inc(s["w_hi"], 1)
                with act.Fori(0, NGR // 2) as it:
                    for b in range(2):
                        for e in range(EG):
                            split(it, b, e)

            @block.vector
            def _(dve):
                def weigh(it, b, e):
                    n = it * 2 * EG + b * EG + e
                    dve.wait_ge(s_a[e % 4], (it * 4 + b * 2 + e // 4 + 1) * 16)
                    if e % 4 == 0:
                        dve.wait_ge(s_g[e // 4], (it * 2 + b + 1) * 16)
                    if e == 0:
                        dve.wait_ge(s["down"], it * 2 * KD + b * KD + 1)
                    tok = "p (b t) -> p b t"
                    nc.vector.tensor_tensor(wf[:, e % 2, :].rearrange(tok, t=GTOK), abuf[:, e % 4, :].rearrange(tok, t=GTOK),
                                            gbuf[:, e // 4, :, (e % 4) * GTOK:(e % 4 + 1) * GTOK], ALU.mult).then_inc(s["w"], 1)
                    dve.wait_ge(s["v_hi"], n + 1)
                    nc.vector.tensor_tensor(vl[:, b, e, :], vraw[:, e % 4, :], vh[:, b, e, :], ALU.subtract).then_inc(s["v_lo"], 1)
                    dve.wait_ge(s["w_hi"], n + 1)
                    nc.vector.tensor_tensor(wl[:, b, e, :], wf[:, e % 2, :], wh[:, b, e, :], ALU.subtract).then_inc(s["w_lo"], 1)

                def add(it, b, d):
                    n = it * 2 * KD + b * KD + d
                    dve.wait_ge(s["down"], n + KD + 1)
                    dve.wait_ge(s["sum"], n + 1)
                    y = k.acc[:, d, :].rearrange("p (h c) -> p h c", h=2)
                    nc.vector.tensor_tensor(y, y, psY[:, d % 4, :, 0:HALF], ALU.add).then_inc(s["sum"], 1)

                nc.vector.memset(k.acc[:, :, :], 0.0).then_inc(s["zero"], 1)
                dve.wait_ge(s["zero"], 1)
                dve.sem_inc(s["sum"], 4)
                for e in range(EG):
                    weigh(0, 0, e)
                with dve.Fori(0, NGR // 2 - 1) as it:
                    for b in range(2):
                        for e in range(EG):
                            weigh(it if b == 0 else it + 1, 1 - b, e)
                            add(it, b, e)
                last = NGR // 2 - 1
                for e in range(EG):
                    weigh(last, 1, e)
                    add(last, 0, e)
                for e in range(EG):
                    add(last, 1, e)
                dve.wait_ge(s["sum"], NGR * KD + 4)

            @block.tensor
            def _(pe):
                pe.sem_inc(s["down"], KD)
                with pe.Fori(0, NGR // 2) as it:
                    for b in range(2):
                        pe.wait_ge(s["v_lo"], it * 2 * EG + b * EG + EG)
                        pe.wait_ge(s["w_lo"], it * 2 * EG + b * EG + EG)
                        for d in range(KD):
                            n = it * 2 * KD + b * KD + d
                            pe.wait_ge(s["sum"], n + 1)
                            for e in range(EG):
                                for v, ws in ((vh, (wh, wl)), (vl, (wh,))):
                                    for m, w in enumerate(ws):
                                        for hf in range(2):
                                            mm = nc.tensor.matmul(psY[:, d % 4, hf, 0:HALF], v[:, b, e, d * P:(d + 1) * P],
                                                                  w[:, b, e, hf * HALF:(hf + 1) * HALF],
                                                                  start=(e == 0 and v is vh and m == 0),
                                                                  stop=(e == EG - 1 and v is vl))
                            mm.then_inc(s["down"], 1)


def output_phase(nc, k, sem):
    names = ("scaled", "turned", "added", "stored")
    s = {n: sem("out_" + n) for n in names}
    with ExitStack() as ctx:
        ps = ctx.enter_context(nc.psum_tensor("psOut", [P, 4, 2, 512], F32))
        with nc.Block() as block:
            @block.vector
            def _(dve):
                for d in range(KD):
                    for g, (g0, gw) in enumerate(GROUP_COLS):
                        nc.vector.tensor_scalar(k.acc[:, d, g0:g0 + gw], k.acc[:, d, g0:g0 + gw],
                                                k.mod[:, 40 + d, g:g + 1], None, ALU.mult).then_inc(s["scaled"], 1)
                for i, (t0, w) in enumerate(TT):
                    dve.wait_ge(s["turned"], i + 1)
                    xv = k.x[0:w, i, :].rearrange("p (h c) -> p h c", h=2)
                    nc.vector.tensor_tensor(xv, xv, ps[0:w, i % 4, :, :], ALU.add).then_inc(s["added"], 1)

            @block.tensor
            def _(pe):
                pe.wait_ge(s["scaled"], 2 * KD)
                for i, (t0, w) in enumerate(TT):
                    if i == 4:
                        pe.wait_ge(s["added"], 1)
                    for d in range(KD):
                        mm = nc.tensor.transpose(ps[0:w, i % 4, d // 4, (d % 4) * P:(d % 4 + 1) * P],
                                                 k.acc[:, d, t0:t0 + w], k.ident[:, :])
                    mm.then_inc(s["turned"], 1)

            @block.sync
            def _(sp):
                for i, (t0, w) in enumerate(TT):
                    sp.wait_ge(s["added"], i + 1)
                    dst = k.o_y_p[0, t0:t0 + w, :] if i < 4 else k.o_y_s[0]
                    sp.dma_start(dst, k.x[0:w, i, :]).then_inc(s["stored"], 16)
                sp.wait_ge(s["stored"], 16 * NTT)


_INS = ['x_prompt', 'c_prompt', 'x_sample', 'c_sample', 'cache_k', 'cache_v', 'cache_conv', 'w_ada', 'b_ada',
        'norm1_gain', 'norm2_gain', 'w_in', 'q_gain', 'k_gain', 'rel_table', 'conv_w', 'w_o_att', 'w_o_conv',
        'w_o', 'w_pq', 'sub_keys1', 'sub_keys2', 'expert_u', 'expert_v']


_OUTS = [("o_y_p", (1, 512, 1024)), ("o_y_s", (1, 64, 1024)),
         ("o_k_p", (1, 1, 512, 8, 64)), ("o_v_p", (1, 1, 512, 8, 64)), ("o_conv_p", (1, 1, 2, 512)),
         ("o_k_s", (1, 1, 64, 8, 64)), ("o_v_s", (1, 1, 64, 8, 64)), ("o_conv_s", (1, 1, 2, 512))]


def program(nc, ins, outs):
    k = Kernel()
    k.x_prompt = ins["x_prompt"]
    k.c_prompt = ins["c_prompt"]
    k.x_sample = ins["x_sample"]
    k.c_sample = ins["c_sample"]
    k.cache_k = ins["cache_k"]
    k.cache_v = ins["cache_v"]
    k.cache_conv = ins["cache_conv"]
    k.w_ada = ins["w_ada"]
    k.b_ada = ins["b_ada"]
    k.norm1_gain = ins["norm1_gain"]
    k.norm2_gain = ins["norm2_gain"]
    k.w_in = ins["w_in"]
    k.q_gain = ins["q_gain"]
    k.k_gain = ins["k_gain"]
    k.rel_table = ins["rel_table"]
    k.conv_w = ins["conv_w"]
    k.w_o_att = ins["w_o_att"]
    k.w_o_conv = ins["w_o_conv"]
    k.w_o = ins["w_o"]
    k.w_pq = ins["w_pq"]
    k.sub_keys1 = ins["sub_keys1"]
    k.sub_keys2 = ins["sub_keys2"]
    k.expert_u = ins["expert_u"]
    k.expert_v = ins["expert_v"]
    k.rel_ext = ins["rel_ext"]
    k.gate_dram = ins["gate_dram"]
    k.act_dram = ins["act_dram"]
    k.o_y_p = outs["o_y_p"]
    k.o_y_s = outs["o_y_s"]
    k.o_k_p = outs["o_k_p"]
    k.o_v_p = outs["o_v_p"]
    k.o_conv_p = outs["o_conv_p"]
    k.o_k_s = outs["o_k_s"]
    k.o_v_s = outs["o_v_s"]
    k.o_conv_s = outs["o_conv_s"]
    with ExitStack() as ctx:
        def sb(name, shape, dt=F32):
            return ctx.enter_context(nc.sbuf_tensor(name, shape, dt))

        def sem(name):
            return ctx.enter_context(nc.semaphore(name))
        k.x = sb("x", [P, NTT, D])
        k.ident = sb("ident", [P, P])
        k.flip = sb("flip", [P, P])
        k.blk64 = sb("blk64", [P, P])
        k.vT = sb("vT", [P, NVEC])
        k.siluc = sb("siluc", [P, KD, 2])
        k.mod = sb("mod", [P, 48, 2])
        k.fac = sb("fac", [P, 2, KD, 2])
        k.s_x = [sem(f"x_loaded{i}") for i in range(NTT)]
        k.s_ring = [sem(f"ring_free{i}") for i in range(3)]
        with ExitStack() as front:
            k.zT = front.enter_context(nc.sbuf_tensor("zT", [P, 40, T], F32))
            k.wring = front.enter_context(nc.sbuf_tensor("wring", [P, 3, WBLK], F32))
            setup_phase(nc, k, sem)
            with ExitStack() as hs:
                k.hT = hs.enter_context(nc.sbuf_tensor("hT", [P, KD, T], F32))
                ada_phase(nc, k, sem)
                z_phase(nc, k, sem)
            with ExitStack() as att:
                k.bias = att.enter_context(nc.sbuf_tensor("bias", [P, NHEAD, 256], F32))
                k.kcT = att.enter_context(nc.sbuf_tensor("kcT", [P, 4, P], F32))
                k.cv = att.enter_context(nc.sbuf_tensor("cv", [P, ATT], F32))
                prep_phase(nc, k, sem)
                attention_phase(nc, k, sem)
            merge_phase(nc, k, sem)
        with ExitStack() as mid:
            def sbm(name, shape, dt=F32):
                return mid.enter_context(nc.sbuf_tensor(name, shape, dt))
            k.h2hi = sbm("h2hi", [P, KD, T], BF16)
            k.h2lo = sbm("h2lo", [P, KD, T], BF16)
            k.pairs = sbm("pairs", [P, 4, TPAD])
            k.iota128 = sbm("iota128", [P, P], BF16)
            with ExitStack() as tk:
                k.h2T = tk.enter_context(nc.sbuf_tensor("h2T", [P, KD, TPAD], F32))
                k.wpq = tk.enter_context(nc.sbuf_tensor("wpq", [P, KD, 2 * PH * P], F32))
                k.subk = tk.enter_context(nc.sbuf_tensor("subk", [P, PH, 2, NKEY], F32))
                k.s_wpq = sem("w_pq_loaded")
                k.s_subk = sem("sub_keys_loaded")
                norm2_phase(nc, k, sem)
                topk_phase(nc, k, sem)
            gates_phase(nc, k, sem)
            up_phase(nc, k, sem)
        k.acc = sb("acc", [P, KD, T])
        down_phase(nc, k, sem)
        output_phase(nc, k, sem)


def kernel(**inputs):
    import numpy as _np
    import concourse.bacc as _bacc
    from concourse import mybir as _mybir
    from concourse.bass_utils import run_bass_kernel_spmd as _run
    nc = _bacc.Bacc("TRN2", target_bir_lowering=False, num_devices=1)
    arrays, ins = {}, {}
    for name in _INS:
        a = _np.ascontiguousarray(inputs[name])
        arrays[f"in_{name}_dram"] = a
        ins[name] = nc.dram_tensor(f"in_{name}_dram", a.shape, _mybir.dt.from_np(a.dtype), kind="ExternalInput").ap()
    f32 = _mybir.dt.float32
    ins["rel_ext"] = nc.dram_tensor("rel_ext", (8, 384), f32).ap()
    outs = {n: nc.dram_tensor(n, s, f32, kind="ExternalOutput").ap() for n, s in _OUTS}
    ins["gate_dram"] = nc.dram_tensor("gate_scratch", (NGB, P, P, GTOK), f32).ap()
    ins["act_dram"] = nc.dram_tensor("act_scratch", (NEXP // P, P, T), f32).ap()
    program(nc, ins, outs)
    r = _run(nc, [arrays], core_ids=[0])
    return tuple(r.results[0][n] for n, _ in _OUTS)
```

```python
from contextlib import ExitStack

import concourse.bass as bass
from concourse import mybir

ALU = mybir.AluOpType
ACT = mybir.ActivationFunctionType
AX_X = mybir.AxisListType.X
F32 = mybir.dt.float32
BF16 = mybir.dt.bfloat16
U32 = mybir.dt.uint32
ds = bass.ds

P = 128
D = 1024
KD = D // P
TP = 512
TS = 64
T = TP + TS
HALF = T // 2
NTT = 5
TT = [(128 * i, 128) for i in range(4)] + [(TP, TS)]
GROUP_COLS = [(0, TP), (TP, TS)]
NHEAD = 8
HD = 64
ATT = NHEAD * HD
CONV = 512
CT = CONV // P
PAST = 128
NREL = 257
PH = 8
NKEY = 128
TOPK = 16
NEXP = NKEY * NKEY
EPS = 1e-6
WBLK = 4096
TPAD = NTT * P
GTOK = 32
NGB = T // GTOK
EG = 8

C_BADA, C_G1, C_G2, C_CW, C_CC, C_QG, C_KG, C_C = 0, 48, 56, 64, 76, 84, 85, 86
NVEC = 102
Z_Q, Z_K, Z_V, Z_B, Z_C, Z_X, Z_GA, Z_GC = 0, 4, 8, 12, 16, 20, 24, 32


class Kernel:
    pass


def bc(ap, axis, n):
    wide = ap.unsqueeze(axis)
    shape = list(wide.shape)
    shape[axis] = n
    return wide.to_broadcast(shape)


class Chain:

    def __init__(self, sem, it=0, per=0, start=0):
        self.sem, self.base, self.per, self.n = sem, start + (it * per if per else 0), per, 0

    def did(self, ins):
        ins.then_inc(self.sem, 1)
        self.n += 1
        return self.n

    def at(self, n=None):
        return self.base + (self.n if n is None else n)

    def end(self):
        assert self.n == self.per, (self.n, self.per)


ADA_SLOT = [2, 0, 1, 2]


def load_ada(eng, k, b, slot):
    eng.dma_start(k.wring[:, slot, :].rearrange("p (t n) -> p t n", t=KD),
                  k.w_ada[0].rearrange("(t p) n -> p t n", p=P)[:, :, b * 512:(b + 1) * 512]).then_inc(k.s_ada[b], 16)


def load_ada_pass(eng, k, it, slot):
    eng.dma_start(k.wring[:, slot, :].rearrange("p (t n) -> p t n", t=KD),
                  k.w_ada[0].rearrange("(t p) n -> p t n", p=P)[:, :, ds(it * 1024 + (4 + slot) * 512, 512)]
                  ).then_inc(k.s_adr[slot], 16)


def setup_phase(nc, k, sem):
    s_vec, s_blk, s_const0, s_const, s_vT, s_vTs, s_silu = (sem(n) for n in (
        "vec_loaded", "blk64_set", "const_zeroed", "const_ready", "vec_turned", "vec_ready", "silu_ready"))
    with ExitStack() as ctx:
        vecs = ctx.enter_context(nc.sbuf_tensor("vecs", [P, P], F32))
        psV = ctx.enter_context(nc.psum_tensor("psV", [P, 512], F32))
        with nc.Block() as block:
            @block.sync
            def _(sp):
                loads = [(vecs[C_BADA:C_BADA + 48, :], k.b_ada.rearrange("l (r c) -> (l r) c", c=P)),
                         (vecs[C_G1:C_G1 + 8, :], k.norm1_gain.rearrange("l (r c) -> (l r) c", c=P)),
                         (vecs[C_G2:C_G2 + 8, :], k.norm2_gain.rearrange("l (r c) -> (l r) c", c=P)),
                         (vecs[C_CW:C_CW + 12, :], k.conv_w.rearrange("l w (r c) -> (l w r) c", c=P)),
                         (vecs[C_CC:C_CC + 8, :], k.cache_conv.rearrange("l b w (r c) -> (l b w r) c", c=P)),
                         (vecs[C_QG:C_QG + 1, 0:HD], k.q_gain), (vecs[C_QG:C_QG + 1, HD:P], k.q_gain),
                         (vecs[C_KG:C_KG + 1, 0:HD], k.k_gain), (vecs[C_KG:C_KG + 1, HD:P], k.k_gain),
                         (vecs[C_C:C_C + 8, :], k.c_prompt.rearrange("b (r c) -> (b r) c", c=P)),
                         (vecs[C_C + 8:C_C + 16, :], k.c_sample.rearrange("b (r c) -> (b r) c", c=P))]
                for dst, src in loads:
                    sp.dma_start(dst, src).then_inc(s_vec, 16)
                for b in range(3):
                    load_ada(sp, k, b, ADA_SLOT[b])
                for i, (t0, w) in enumerate(TT):
                    src = k.x_prompt[0, t0:t0 + w, :] if i < 4 else k.x_sample[0, :, :]
                    sp.dma_start(k.x[0:w, i, :], src).then_inc(k.s_x[i], 16)

            @block.gpsimd
            def _(pool):
                nc.gpsimd.memset(k.ident[:, :], 0.0).then_inc(s_const0, 1)
                nc.gpsimd.memset(k.flip[:, :], 0.0).then_inc(s_const0, 1)
                pool.wait_ge(s_const0, 2)
                nc.gpsimd.affine_select(out=k.ident[:, :], in_=k.ident[:, :], compare_op=ALU.not_equal, fill=1.0,
                                        base=0, pattern=[[-1, P]], channel_multiplier=1).then_inc(s_const, 1)
                nc.gpsimd.affine_select(out=k.flip[:, :], in_=k.flip[:, :], compare_op=ALU.not_equal, fill=1.0,
                                        base=-(P - 1), pattern=[[1, P]], channel_multiplier=1).then_inc(s_const, 1)
                pool.wait_ge(s_const, 2)

            @block.tensor
            def _(pe):
                pe.wait_ge(s_vec, 16 * 11)
                pe.wait_ge(s_const, 2)
                nc.tensor.transpose(psV[:, 0:NVEC], vecs[0:NVEC, :], k.ident[0:NVEC, 0:NVEC]).then_inc(s_vT, 1)

            @block.vector
            def _(dve):
                nc.vector.memset(k.blk64[:, :], 0.0).then_inc(s_blk, 1)
                dve.wait_ge(s_blk, 1)
                for a in range(2):
                    nc.vector.memset(k.blk64[a * HD:(a + 1) * HD, a * HD:(a + 1) * HD], 1.0).then_inc(s_blk, 1)
                dve.wait_ge(s_vT, 1)
                nc.vector.tensor_copy(k.vT[:, 0:NVEC], psV[:, 0:NVEC]).then_inc(s_vTs, 1)

            @block.scalar
            def _(act):
                act.wait_ge(s_vTs, 1)
                nc.scalar.activation(k.siluc[:, :, :], k.vT[:, C_C:C_C + 16].rearrange("p (g t) -> p t g", g=2),
                                     ACT.Silu).then_inc(s_silu, 1)
                act.wait_ge(s_silu, 1)


def ada_block(nc, k, pe, psM, slot):
    w = k.wring[:, slot, :].rearrange("p (t n) -> p t n", t=KD)
    for t in range(KD):
        mm = nc.tensor.matmul(psM[0:2, 0:512], k.siluc[:, t, :], w[:, t, :], start=(t == 0), stop=(t == KD - 1))
    return mm


def ada_phase(nc, k, sem):
    s_row, s_rows, s_col, s_mod, s_sq, s_r, s_rc, s_rs, s_xn, s_tp, s_hd, s_ha, s_ab = (sem(n) for n in (
        "ada_row", "ada_row_kept", "ada_col", "ada_mod", "x_squares", "x_mean", "x_inverse", "x_rstd", "xn_ready",
        "xn_turned", "h_ready_dve", "h_ready_act", "ab_ready"))
    with ExitStack() as ctx:
        sq = ctx.enter_context(nc.sbuf_tensor("sq", [P, D], F32))
        xn = ctx.enter_context(nc.sbuf_tensor("xn", [P, 2, D], F32))
        st = ctx.enter_context(nc.sbuf_tensor("st", [P, 4, 8], F32))
        mrow = ctx.enter_context(nc.sbuf_tensor("mrow", [2, 2, 512], F32))
        psM = ctx.enter_context(nc.psum_tensor("psM", [P, 2, 512], F32))
        psC = ctx.enter_context(nc.psum_tensor("psCol", [P, 2, 512], F32))
        psT = ctx.enter_context(nc.psum_tensor("psT", [P, 2, KD, P], F32))
        with nc.Block() as block:
            @block.sync
            def _(sp):
                w_in = k.w_in[0].rearrange("(t p) n -> p t n", p=P)
                sp.wait_ge(s_row, 1)
                load_ada(sp, k, 3, 2)
                for s, n in ((0, 2), (1, 3)):
                    sp.wait_ge(s_row, n)
                    sp.dma_start(k.wring[:, s, :].rearrange("p (t n) -> p t n", t=KD),
                                 w_in[:, :, s * 512:(s + 1) * 512]).then_inc(k.s_win[s], 16)

            @block.tensor
            def _(pe):
                for b in range(4):
                    pe.wait_ge(k.s_ada[b], 16)
                    if b >= 2:
                        pe.wait_ge(s_rows, b - 1)
                    ada_block(nc, k, pe, psM[:, b % 2, :], ADA_SLOT[b]).then_inc(s_row, 1)
                    pe.wait_ge(s_rows, b + 1)
                    if b >= 2:
                        pe.wait_ge(s_mod, b - 1)
                    for c in range(4):
                        mm = nc.tensor.transpose(psC[:, b % 2, 2 * c:2 * c + 2], mrow[:, b % 2, c * P:(c + 1) * P],
                                                 k.ident[0:2, 0:2])
                    mm.then_inc(s_col, 1)
                for i, (t0, w) in enumerate(TT):
                    pe.wait_ge(s_xn, i + 1)
                    if i >= 2:
                        pe.wait_ge(s_hd, KD // 2 * (i - 1))
                        pe.wait_ge(s_ha, KD // 2 * (i - 1))
                    for t in range(KD):
                        mm = nc.tensor.transpose(psT[:, i % 2, t, 0:w], xn[0:w, i % 2, t * P:(t + 1) * P],
                                                 k.ident[0:w, 0:w])
                    mm.then_inc(s_tp, 1)

            @block.vector
            def _(dve):
                for i, (t0, w) in enumerate(TT):
                    dve.wait_ge(s_sq, i + 1)
                    nc.vector.tensor_scalar(st[0:w, 1, i:i + 1], st[0:w, 0, i:i + 1], 1.0 / D, EPS,
                                            ALU.mult, ALU.add).then_inc(s_r, 1)
                    dve.wait_ge(s_r, i + 1)
                    nc.vector.reciprocal(st[0:w, 2, i:i + 1], st[0:w, 1, i:i + 1]).then_inc(s_rc, 1)
                    if i < 2:
                        dve.wait_ge(s_rs, i + 1)
                        nc.vector.tensor_scalar(xn[0:w, i, :], k.x[0:w, i, :], st[0:w, 3, i:i + 1], None,
                                                ALU.mult).then_inc(s_xn, 1)
                for b in range(4):
                    dve.wait_ge(s_row, b + 1)
                    if b >= 2:
                        dve.wait_ge(s_col, b - 1)
                    nc.vector.tensor_copy(mrow[:, b % 2, :], psM[0:2, b % 2, :]).then_inc(s_rows, 1)
                    dve.wait_ge(s_col, b + 1)
                    nc.vector.tensor_tensor(k.mod[:, 4 * b:4 * b + 4, :],
                                            psC[:, b % 2, 0:8].rearrange("p (j g) -> p j g", g=2),
                                            bc(k.vT[:, C_BADA + 4 * b:C_BADA + 4 * b + 4], 2, 2), ALU.add).then_inc(s_mod, 1)
                dve.wait_ge(s_mod, 4)
                nc.vector.tensor_scalar(k.fac[:, 0, :, :], k.mod[:, 8:16, :], 1.0, None, ALU.add).then_inc(s_ab, 1)
                dve.wait_ge(s_ab, 1)
                nc.vector.tensor_tensor(k.fac[:, 0, :, :], k.fac[:, 0, :, :],
                                        bc(k.vT[:, C_G1:C_G1 + 8], 2, 2), ALU.mult).then_inc(s_ab, 1)
                dve.wait_ge(s_ab, 2)
                for i, (t0, w) in enumerate(TT):
                    g = i // 4
                    dve.wait_ge(s_tp, i + 1)
                    for t in range(KD // 2):
                        nc.vector.tensor_scalar(k.hT[:, t, t0:t0 + w], psT[:, i % 2, t, 0:w], k.fac[:, 0, t, g:g + 1],
                                                k.mod[:, t, g:g + 1], ALU.mult, ALU.add).then_inc(s_hd, 1)
                    if i + 2 < NTT:
                        w2 = TT[i + 2][1]
                        dve.wait_ge(s_rs, i + 3)
                        nc.vector.tensor_scalar(xn[0:w2, i % 2, :], k.x[0:w2, i + 2, :], st[0:w2, 3, i + 2:i + 3], None,
                                                ALU.mult).then_inc(s_xn, 1)

            @block.scalar
            def _(act):
                for i, (t0, w) in enumerate(TT):
                    act.wait_ge(k.s_x[i], 16)
                    if i:
                        act.wait_ge(s_sq, i)
                    nc.scalar.activation(sq[0:w, :], k.x[0:w, i, :], ACT.Square,
                                         accum_out=st[0:w, 0, i:i + 1]).then_inc(s_sq, 1)
                for i, (t0, w) in enumerate(TT):
                    act.wait_ge(s_rc, i + 1)
                    nc.scalar.activation(st[0:w, 3, i:i + 1], st[0:w, 2, i:i + 1], ACT.Sqrt).then_inc(s_rs, 1)
                act.wait_ge(s_ab, 2)
                for i, (t0, w) in enumerate(TT):
                    g = i // 4
                    act.wait_ge(s_tp, i + 1)
                    for t in range(KD // 2, KD):
                        nc.scalar.activation(k.hT[:, t, t0:t0 + w], psT[:, i % 2, t, 0:w], ACT.Identity,
                                             bias=k.mod[:, t, g:g + 1], scale=k.fac[:, 0, t, g:g + 1]).then_inc(s_ha, 1)


def z_phase(nc, k, sem):
    s_w = k.s_win
    s_used = [sem(f"win_used{i}") for i in range(2)]
    s_z, s_za, s_zd = sem("z_tile_done"), sem("z_evicted_act"), sem("z_evicted_dve")
    with ExitStack() as ctx:
        psZ = ctx.enter_context(nc.psum_tensor("psZ", [P, 8, 512], F32))
        with nc.Block() as block:
            @block.sync
            def _(sp):
                w_in = k.w_in[0].rearrange("(t p) n -> p t n", p=P)

                def load(s, col):
                    sp.dma_start(k.wring[:, s, :].rearrange("p (t n) -> p t n", t=KD),
                                 w_in[:, :, ds(col, 512)]).then_inc(s_w[s], 16)
                with sp.Fori(1, 5) as it:
                    for s in range(2):
                        sp.wait_ge(s_used[s], it)
                        load(s, (it * 2 + s) * 512)

            @block.tensor
            def _(pe):
                with pe.Fori(0, 5) as it:
                    for s in range(2):
                        pe.wait_ge(s_w[s], (it + 1) * 16)
                        w = k.wring[:, s, :].rearrange("p (t n) -> p t n", t=KD)
                        for c in range(4):
                            pe.wait_ge(s_za, it * 8 + 4 * s + c + 1)
                            pe.wait_ge(s_zd, it * 8 + 4 * s + c + 1)
                            for t in range(KD):
                                for hf in range(2):
                                    mm = nc.tensor.matmul(psZ[:, 2 * c + hf, 0:HALF], w[:, t, c * P:(c + 1) * P],
                                                          k.hT[:, t, hf * HALF:(hf + 1) * HALF],
                                                          start=(t == 0), stop=(t == KD - 1))
                            mm.then_inc(s_z, 1)
                        pe.wait_ge(s_z, it * 8 + 4 * s + 4)
                        pe.sem_inc(s_used[s], 1)

            def evict(eng, copy, hf, s_out):
                eng.sem_inc(s_out, 4)
                with eng.Fori(0, 10) as it:
                    for c in range(4):
                        eng.wait_ge(s_z, it * 4 + c + 1)
                        copy(k.zT[:, ds(it * 4 + c, 1), hf * HALF:(hf + 1) * HALF],
                             psZ[:, 2 * c + hf:2 * c + hf + 1, 0:HALF]).then_inc(s_out, 1)

            @block.scalar
            def _(act):
                evict(act, nc.scalar.copy, 0, s_za)

            @block.vector
            def _(dve):
                evict(dve, lambda o, i: nc.vector.tensor_scalar(o, i, 1.0, None, ALU.mult), 1, s_zd)


def prep_phase(nc, k, sem):
    s_rel, s_ext, s_extd, s_tt, s_flip, s_bias = (sem(n) for n in (
        "rel_loaded", "rel_extended", "rel_in_dram", "rel_diagonals", "bias_flipped", "bias_ready"))
    s_ck, s_cv, s_kt, s_u, s_cv1, s_st, s_sT, s_so, s_out = (sem(n) for n in (
        "cache_k_loaded", "cache_v_loaded", "cache_k_turned", "conv_input", "conv_step", "conv_state", "conv_state_turned",
        "conv_state_ready", "conv_state_stored"))
    NX = 384
    with ExitStack() as ctx:
        def sb(name, shape):
            return ctx.enter_context(nc.sbuf_tensor(name, shape, F32))
        rel = sb("rel", [NHEAD, NREL])
        ext = sb("ext", [NHEAD, NX])
        diag = sb("diag", [P, NHEAD, 256])
        ck = sb("ck", [P, ATT])
        ubuf = sb("ubuf", [P, CT, T + 4])
        ybuf = sb("ybuf", [P, T + 2])
        cst = sb("cst", [P, 16])
        cso = sb("cso", [16, P])
        psB = ctx.enter_context(nc.psum_tensor("psB", [P, 4, 512], F32))
        psK = ctx.enter_context(nc.psum_tensor("psK", [P, 512], F32))
        psC = ctx.enter_context(nc.psum_tensor("psC", [P, 512], F32))
        with nc.Block() as block:
            @block.sync
            def _(sp):
                sp.dma_start(rel[:, :], k.rel_table[0]).then_inc(s_rel, 16)
                for slot in range(2):
                    load_ada_pass(sp, k, 0, slot)
                sp.dma_start(k.wring[:, 2, :].rearrange("p (t n) -> p t n", t=KD),
                             k.w_o[0].rearrange("(t p) n -> p t n", p=P)[:, :, 0:512]).then_inc(k.s_mg[2], 16)
                sp.dma_start(ck[:, :], k.cache_k[0, 0].rearrange("t h d -> t (h d)")).then_inc(s_ck, 16)
                sp.dma_start(k.cv[:, :], k.cache_v[0, 0].rearrange("t h d -> t (h d)")).then_inc(s_cv, 16)
                sp.wait_ge(s_ext, 2)
                sp.dma_start(k.rel_ext, ext[:, :]).then_inc(s_extd, 16)
                sp.wait_ge(s_extd, 16)
                src = bass.AP(k.rel_ext.tensor, 0, [[1, P], [NX, NHEAD], [1, 256]])
                sp.dma_start(diag[:, :, :], src).then_inc(s_tt, 16)
                sp.wait_ge(s_so, 1)
                for g, o in enumerate((k.o_conv_p, k.o_conv_s)):
                    sp.dma_start(o.rearrange("l b w (r c) -> (l b w r) c", c=P), cso[8 * g:8 * g + 8, :]).then_inc(s_out, 16)
                sp.wait_ge(s_cv, 16)
                sp.wait_ge(s_out, 32)

            @block.tensor
            def _(pe):
                pe.wait_ge(s_ck, 16)
                for c in range(4):
                    mm = nc.tensor.transpose(psK[:, c * P:(c + 1) * P], ck[:, c * P:(c + 1) * P], k.ident[:, :])
                mm.then_inc(s_kt, 1)
                pe.wait_ge(s_tt, 16)
                for h in range(NHEAD):
                    for o in range(2):
                        mm = nc.tensor.matmul(psB[:, h // 2, (h % 2) * 256 + (1 - o) * P:(h % 2) * 256 + (2 - o) * P],
                                              diag[:, h, o * P:(o + 1) * P], k.flip[:, :], start=True, stop=True)
                mm.then_inc(s_flip, 1)
                pe.wait_ge(s_st, 1)
                nc.tensor.transpose(psC[0:16, 0:P], cst[:, :], k.ident[:, :]).then_inc(s_sT, 1)

            @block.scalar
            def _(act):
                act.wait_ge(s_kt, 1)
                nc.scalar.copy(k.kcT[:, :, :], psK[:, :].rearrange("p (c t) -> p c t", c=4)).then_inc(s_bias, 1)
                act.wait_ge(s_flip, 1)
                for b in range(4):
                    nc.scalar.copy(k.bias[:, 2 * b:2 * b + 2, :], psB[:, b, :].rearrange("p (h m) -> p h m", h=2)).then_inc(s_bias, 1)
                act.wait_ge(s_bias, 5)

            @block.vector
            def _(dve):
                dve.wait_ge(s_rel, 16)
                nc.vector.tensor_copy(ext[:, 0:256], rel[:, 1:257]).then_inc(s_ext, 1)
                nc.vector.tensor_copy(ext[:, 256:NX], rel[:, 256:257].to_broadcast([NHEAD, NX - 256])).then_inc(s_ext, 1)
                nc.vector.memset(ubuf[:, :, 0:2], 0.0).then_inc(s_u, 1)
                nc.vector.tensor_copy(ubuf[:, :, TP + 2:TP + 4],
                                      k.vT[:, C_CC:C_CC + 8].rearrange("p (w c) -> p c w", w=2)).then_inc(s_u, 1)
                for (g0, gw), u0 in zip(GROUP_COLS, (2, TP + 4)):
                    nc.vector.tensor_tensor(ubuf[:, :, u0:u0 + gw], k.zT[:, Z_C:Z_C + CT, g0:g0 + gw],
                                            k.zT[:, Z_X:Z_X + CT, g0:g0 + gw], ALU.mult).then_inc(s_u, 1)
                dve.wait_ge(s_u, 4)
                for g, u0 in enumerate((TP, TP + 2 + TS)):
                    nc.vector.tensor_copy(cst[:, 8 * g:8 * g + 8].rearrange("p (w c) -> p c w", w=2),
                                          ubuf[:, :, u0:u0 + 2]).then_inc(s_u, 1)
                dve.wait_ge(s_u, 6)
                dve.sem_inc(s_st, 1)
                n = Chain(s_cv1)
                for c in range(CT):
                    for w in range(3):
                        wcol = k.vT[:, C_CW + w * CT + c:C_CW + w * CT + c + 1]
                        u = ubuf[:, c, w:w + T + 2]
                        if w == 0:
                            n.did(nc.vector.tensor_scalar(ybuf[:, :], u, wcol, None, ALU.mult))
                        else:
                            n.did(nc.vector.scalar_tensor_tensor(ybuf[:, :], u, wcol, ybuf[:, :], ALU.mult, ALU.add))
                        dve.wait_ge(s_cv1, n.at())
                    for (g0, gw), u0 in zip(GROUP_COLS, (0, TP + 2)):
                        n.did(nc.vector.tensor_tensor(k.zT[:, Z_B + c, g0:g0 + gw], k.zT[:, Z_B + c, g0:g0 + gw],
                                                      ybuf[:, u0:u0 + gw], ALU.mult))
                    dve.wait_ge(s_cv1, n.at())
                dve.wait_ge(s_sT, 1)
                nc.vector.tensor_copy(cso[:, :], psC[0:16, 0:P]).then_inc(s_so, 1)


def attention_phase(nc, k, sem):
    names = ("sq_ready", "sums_ready", "inverse_ready", "root_ready", "normed_ready", "v_staged", "v_turned", "v_ready",
             "k_turned", "k_natural", "kv_stored", "scores_ready", "max_ready", "exp_ready", "probs_ready",
             "probs_turned", "probsT_ready", "out_ready", "out_stored", "dve_step",
             "row", "row_kept", "col", "mod")
    s = {n: sem("att_" + n) for n in names}
    NU = 10
    units = [(i, hh) for i in range(NTT) for hh in range(2)]
    NDVE = 4 + 2 * (3 + 3 + 4 + 4 + 2)
    with ExitStack() as ctx:
        def sb(name, shape):
            return ctx.enter_context(nc.sbuf_tensor(name, shape, F32))
        qk = sb("qk", [P, 2, TPAD])
        nsc = sb("nsc", [P, T])
        vst = sb("vst", [P, T])
        kcs = sb("kcs", [P, P])
        cvs = sb("cvs", [P, P])
        vn = sb("vn", [P, NTT, P])
        kn = sb("kn", [P, NTT, P])
        sc = sb("sc", [P, 2, 512])
        pT = sb("pT", [P, 2, 512])
        stat = sb("stat", [P, 2, 4])
        mrow = sb("mrow2", [2, 512])
        psN = ctx.enter_context(nc.psum_tensor("psN", [P, 2, 512], F32))
        psS = ctx.enter_context(nc.psum_tensor("psS", [P, 2, 512], F32))
        psP = ctx.enter_context(nc.psum_tensor("psP", [P, 2, 512], F32))
        psO = ctx.enter_context(nc.psum_tensor("psO", [P, 2, 512], F32))

        def keys(i):
            return 128 * (i + 1) if i < 4 else PAST + TS

        def ktiles(i):
            return [(P, j * P) for j in range(i + 1)] if i < 4 else [(P, 0), (TS, P)]

        def done(it, u):
            return it * NU + u + 3

        def freed(it, u):
            return it * NU + u + 1

        with nc.Block() as block:
            @block.sync
            def _(sp):
                sp.sem_inc(s["kv_stored"], 64)
                def rows_out(it, following):
                    col = sp.snap(it * P) if following else it * P
                    for src, ready, op, osm in ((vn, s["v_ready"], k.o_v_p, k.o_v_s), (kn, s["k_natural"], k.o_k_p, k.o_k_s)):
                        sp.wait_ge(ready, it * 2 + 4)
                        sp.dma_start(op[0, 0].rearrange("(i p) h d -> p i (h d)", p=P)[:, :, ds(col, P)],
                                     src[:, 0:4, :]).then_inc(s["kv_stored"], 16)
                        sp.dma_start(osm[0, 0].rearrange("t h d -> t (h d)")[:, ds(col, P)],
                                     src[0:TS, 4, :]).then_inc(s["kv_stored"], 16)
                    if following:
                        for slot in range(2):
                            sp.wait_ge(s["row"], it * 2 + (slot + 1))
                            load_ada_pass(sp, k, it + 1, slot)

                with sp.Fori(0, 3) as it:
                    rows_out(it, True)
                rows_out(3, False)
                for slot, w in enumerate((k.w_o_att, k.w_o_conv)):
                    sp.wait_ge(s["row"], 7 + slot)
                    sp.dma_start(k.wring[:, slot, :].rearrange("p (t n) -> p t n", t=4),
                                 w[0].rearrange("(t p) n -> p t n", p=P)).then_inc(k.s_mg[slot], 16)
                sp.wait_ge(s["kv_stored"], 5 * 64)

            @block.tensor
            def _(pe):
                pe.sem_inc(s["scores_ready"], 2)
                pe.sem_inc(s["col"], 1)
                pe.sem_inc(s["probs_turned"], 2)
                pe.sem_inc(s["out_ready"], 2)
                pe.sem_inc(s["k_turned"], 2)

                def scores(it, u):
                    i, hh = units[u]
                    t0, w = TT[i][0], P
                    h0 = hh * HD
                    pe.wait_ge(s["max_ready"], freed(it, u))
                    q = qk[h0:h0 + HD, 0, t0:t0 + w]
                    if i < 4:
                        mm = nc.tensor.matmul(psS[0:w, u % 2, 0:keys(i)], q, qk[h0:h0 + HD, 1, 0:keys(i)],
                                              start=True, stop=True)
                    else:
                        nc.tensor.matmul(psS[0:w, u % 2, 0:PAST], q, kcs[h0:h0 + HD, :], start=True, stop=True)
                        mm = nc.tensor.matmul(psS[0:w, u % 2, PAST:PAST + TS], q, qk[h0:h0 + HD, 1, TP:T],
                                              start=True, stop=True)
                    mm.then_inc(s["scores_ready"], 1)

                def turn(it, u):
                    i, hh = units[u]
                    w = P
                    pe.wait_ge(s["probs_ready"], done(it, u))
                    pe.wait_ge(s["probsT_ready"], freed(it, u))
                    for n, (kw, k0) in enumerate(ktiles(i)):
                        mm = nc.tensor.transpose(psP[0:kw, u % 2, n * P:n * P + w], sc[0:w, u % 2, k0:k0 + kw],
                                                 k.ident[0:w, 0:w])
                    mm.then_inc(s["probs_turned"], 1)

                def values(it, u):
                    i, hh = units[u]
                    w = P
                    pe.wait_ge(s["probsT_ready"], done(it, u))
                    pe.wait_ge(s["out_stored"], freed(it, u))
                    tiles = ktiles(i)
                    for n, (kw, k0) in enumerate(tiles):
                        v = vn[0:kw, n, :] if i < 4 else (cvs[:, :] if n == 0 else vn[0:kw, 4, :])
                        mm = nc.tensor.matmul(psO[:, u % 2, 0:w], v, pT[0:kw, u % 2, n * P:n * P + w],
                                              start=(n == 0), stop=(n == len(tiles) - 1))
                    mm.then_inc(s["out_ready"], 1)

                with pe.Fori(0, 4) as it:
                    for n in range(2):
                        pe.wait_ge(s["sq_ready"], it * 2 + n + 1)
                        if n == 0:
                            pe.wait_ge(s["k_natural"], it * 2 + 2)
                            pe.wait_ge(s["mod"], it * 2 + 1)
                        else:
                            pe.wait_ge(s["dve_step"], it * NDVE + 2)
                        for hf in range(2):
                            mm = nc.tensor.matmul(psN[:, hf, 0:HALF], k.blk64[:, :], nsc[:, hf * HALF:(hf + 1) * HALF],
                                                  start=True, stop=True)
                        mm.then_inc(s["sums_ready"], 1)
                    pe.wait_ge(s["v_staged"], it + 1)
                    pe.wait_ge(s["dve_step"], it * NDVE + 4)
                    for i, (t0, w) in enumerate(TT):
                        mm = nc.tensor.transpose(psN[0:w, i // 4, (i % 4) * P:(i % 4 + 1) * P], vst[:, t0:t0 + w],
                                                 k.ident[:, :])
                    mm.then_inc(s["v_turned"], 1)
                    pe.wait_ge(s["normed_ready"], it * 2 + 3)
                    pe.wait_ge(s["v_ready"], it * 2 + 4)
                    for i, (t0, w) in enumerate(TT):
                        mm = nc.tensor.transpose(psN[0:w, i // 4, (i % 4) * P:(i % 4 + 1) * P], qk[:, 1, t0:t0 + w],
                                                 k.ident[:, :])
                    mm.then_inc(s["k_turned"], 1)
                    scores(it, 0)
                    scores(it, 1)
                    for u in range(NU):
                        turn(it, u)
                        if u:
                            values(it, u - 1)
                        if u in (3, 7):
                            pe.wait_ge(s["row_kept"], it * 2 + (u // 4 + 2))
                            pe.wait_ge(s["mod"], it * 2 + (u // 4 + 1))
                        if u + 2 < NU:
                            scores(it, u + 2)
                        if u in (1, 5):
                            b = u // 4
                            pe.wait_ge(k.s_adr[b], it * 16 + 16)
                            pe.wait_ge(s["k_natural"], it * 2 + 4)
                            pe.wait_ge(s["row_kept"], it * 2 + (b + 1))
                            ada_block(nc, k, pe, psN[:, 0, :], b).then_inc(s["row"], 1)
                        if u in (3, 7):
                            for c in range(4):
                                mm = nc.tensor.transpose(psN[:, 1, 2 * c:2 * c + 2], mrow[:, c * P:(c + 1) * P],
                                                         k.ident[0:2, 0:2])
                            mm.then_inc(s["col"], 1)
                    values(it, NU - 1)

            @block.scalar
            def _(act):
                act.sem_inc(s["exp_ready"], 2)
                act.sem_inc(s["row_kept"], 1)
                act.sem_inc(s["probsT_ready"], 2)
                act.sem_inc(s["v_ready"], 2)
                act.sem_inc(s["k_natural"], 2)

                def exps(it, u):
                    w, nk = P, keys(units[u][0])
                    act.wait_ge(s["max_ready"], done(it, u))
                    nc.scalar.activation(sc[0:w, u % 2, 0:nk], sc[0:w, u % 2, 0:nk], ACT.Exp,
                                         bias=stat[0:w, u % 2, 0:1], accum_out=stat[0:w, u % 2, 1:2]).then_inc(s["exp_ready"], 1)

                def evict(it, u):
                    i = units[u][0]
                    w = P
                    act.wait_ge(s["probs_turned"], done(it, u))
                    act.wait_ge(s["out_ready"], freed(it, u))
                    if i < 4:
                        nc.scalar.copy(pT[:, u % 2, 0:keys(i)], psP[:, u % 2, 0:keys(i)]).then_inc(s["probsT_ready"], 1)
                    else:
                        nc.scalar.copy(pT[:, u % 2, 0:w], psP[:, u % 2, 0:w])
                        nc.scalar.copy(pT[0:TS, u % 2, P:P + w], psP[0:TS, u % 2, P:P + w]).then_inc(s["probsT_ready"], 1)

                with act.Fori(0, 4) as it:
                    act.wait_ge(s["k_turned"], it + 2)
                    nc.scalar.copy(vst[:, :], k.zT[:, ds(it + Z_V, 1), :]).then_inc(s["v_staged"], 1)
                    act.wait_ge(s["out_ready"], it * NU + 2)
                    nc.scalar.copy(kcs[:, :], k.kcT[:, ds(it, 1), :])
                    nc.scalar.copy(cvs[:, :], k.cv[:, ds(it * P, P)])
                    for n, z0 in enumerate((Z_Q, Z_K)):
                        act.wait_ge(s["normed_ready"], it * 2 + n + 1)
                        nc.scalar.square(nsc[:, :], k.zT[:, ds(it + z0, 1), :]).then_inc(s["sq_ready"], 1)
                        act.wait_ge(s["inverse_ready"], it * 2 + n + 1)
                        nc.scalar.sqrt(nsc[:, :], nsc[:, :]).then_inc(s["root_ready"], 1)
                    for src, dst, ready, turned in ((psN, vn, s["v_ready"], s["v_turned"]), (psN, kn, s["k_natural"], s["k_turned"])):
                        act.wait_ge(turned, it + (1 if dst is vn else 3))
                        if dst is vn:
                            act.wait_ge(s["kv_stored"], it * 64 + 64)
                        nc.scalar.copy(dst[:, 0:4, :], psN[:, 0, :].rearrange("p (i c) -> p i c", i=4)).then_inc(ready, 1)
                        nc.scalar.copy(dst[0:TS, 4, :], psN[0:TS, 1, 0:P]).then_inc(ready, 1)
                    exps(it, 0)
                    exps(it, 1)
                    for u in range(NU):
                        evict(it, u)
                        if u + 2 < NU:
                            exps(it, u + 2)
                        if u in (2, 6):
                            b = u // 4
                            act.wait_ge(s["row"], it * 2 + (b + 1))
                            act.wait_ge(s["col"], it * 2 + (b + 1))
                            nc.scalar.copy(mrow[:, :], psN[0:2, 0, :]).then_inc(s["row_kept"], 1)

            @block.vector
            def _(dve):
                dve.sem_inc(s["max_ready"], 2)
                dve.sem_inc(s["mod"], 1)
                dve.sem_inc(s["probs_ready"], 2)
                dve.sem_inc(s["out_stored"], 2)
                nc.vector.memset(qk[:, :, T:TPAD], 0.0).then_inc(s["normed_ready"], 1)

                def bias_max(n, it, u):
                    i, hh = units[u]
                    w, nk = P, keys(i)
                    dve.wait_ge(s["scores_ready"], done(it, u))
                    dve.wait_ge(s["probs_turned"], freed(it, u))
                    first = nk - 256 if 1 <= i < 4 else 0
                    b = k.bias[0:w, ds(it * 2 + hh, 1), :].rearrange("p a m -> p (a m)")
                    if i == 0:
                        b = b[:, P:2 * P]
                    elif i == 4:
                        b = b[:, 0:nk]
                    if first:
                        n.did(nc.vector.tensor_scalar(sc[0:w, u % 2, 0:first], psS[0:w, u % 2, 0:first], HD ** -0.5,
                                                      b[:, 0:1], ALU.mult, ALU.add))
                    n.did(nc.vector.scalar_tensor_tensor(sc[0:w, u % 2, first:nk], psS[0:w, u % 2, first:nk], HD ** -0.5,
                                                         b, ALU.mult, ALU.add))
                    if i < 4:
                        dve.wait_ge(s["dve_step"], n.at())
                        n.did(nc.vector.memset(sc[0:64, u % 2, nk - 64:nk], -1e30))
                    dve.wait_ge(s["dve_step"], n.at())
                    nc.vector.tensor_reduce(stat[0:w, u % 2, 0:1], sc[0:w, u % 2, 0:nk], AX_X, ALU.max,
                                            negate=True).then_inc(s["max_ready"], 1)

                def normalise(n, it, u):
                    w, nk = P, keys(units[u][0])
                    dve.wait_ge(s["exp_ready"], done(it, u))
                    n.did(nc.vector.reciprocal(stat[0:w, u % 2, 2:3], stat[0:w, u % 2, 1:2]))
                    dve.wait_ge(s["dve_step"], n.at())
                    nc.vector.tensor_scalar(sc[0:w, u % 2, 0:nk], sc[0:w, u % 2, 0:nk], stat[0:w, u % 2, 2:3], None,
                                            ALU.mult).then_inc(s["probs_ready"], 1)

                def store(it, u):
                    i, hh = units[u]
                    t0, w = TT[i]
                    dve.wait_ge(s["out_ready"], done(it, u))
                    nc.vector.tensor_scalar(k.zT[hh * HD:(hh + 1) * HD, ds(it, 1), t0:t0 + w],
                                            psO[hh * HD:(hh + 1) * HD, u % 2:u % 2 + 1, 0:w], 1.0, None,
                                            ALU.mult).then_inc(s["out_stored"], 1)

                with dve.Fori(0, 4) as it:
                    n = Chain(s["dve_step"], it, NDVE)
                    for m, (z0, cg) in enumerate(((Z_Q, C_QG), (Z_K, C_KG))):
                        dve.wait_ge(s["sums_ready"], it * 2 + m + 1)
                        for hf in range(2):
                            n.did(nc.vector.tensor_scalar(nsc[:, hf * HALF:(hf + 1) * HALF], psN[:, hf, 0:HALF], 1.0 / HD,
                                                          EPS, ALU.mult, ALU.add))
                        dve.wait_ge(s["dve_step"], n.at())
                        nc.vector.reciprocal(nsc[:, :], nsc[:, :]).then_inc(s["inverse_ready"], 1)
                        dve.wait_ge(s["root_ready"], it * 2 + m + 1)
                        if m == 0:
                            dve.wait_ge(s["scores_ready"], it * NU + 2)
                            dve.wait_ge(s["k_turned"], it + 2)
                        nc.vector.scalar_tensor_tensor(qk[:, m:m + 1, 0:T], k.zT[:, ds(it + z0, 1), :], k.vT[:, cg:cg + 1],
                                                       nsc[:, :].unsqueeze(1), ALU.mult, ALU.mult).then_inc(s["normed_ready"], 1)
                    bias_max(n, it, 0)
                    bias_max(n, it, 1)
                    normalise(n, it, 0)
                    for u in range(NU):
                        if u + 1 < NU:
                            normalise(n, it, u + 1)
                        if u + 2 < NU:
                            bias_max(n, it, u + 2)
                        if u:
                            store(it, u - 1)
                        if u in (4, 8):
                            b = u // 4 - 1
                            dve.wait_ge(s["col"], it * 2 + (b + 2))
                            nc.vector.tensor_tensor(k.mod[:, ds(it * 8 + (16 + 4 * b), 4), :],
                                                    psN[:, 1, 0:8].rearrange("p (j g) -> p j g", g=2),
                                                    bc(k.vT[:, ds(it * 8 + (16 + 4 * b), 4)], 2, 2), ALU.add).then_inc(s["mod"], 1)
                    store(it, NU - 1)
                    n.end()


def merge_phase(nc, k, sem):
    names = ("sig", "branch", "dve", "merged", "mix", "gated_act", "gated_dve", "turned", "x1")
    s = {n: sem("mg_" + n) for n in names}
    s_w = k.s_mg
    with ExitStack() as ctx:
        mT = ctx.enter_context(nc.sbuf_tensor("mT", [P, KD, T], F32))
        tmp = ctx.enter_context(nc.sbuf_tensor("tmp", [P, T], F32))
        ps = ctx.enter_context(nc.psum_tensor("psB4", [P, 8, 512], F32))
        gm = k.zT[:, 0:KD, :]

        def halves(ap):
            return ap.rearrange("p (h c) -> p h c", h=2)

        with nc.Block() as block:
            @block.sync
            def _(sp):
                w_o = k.w_o[0].rearrange("(t p) n -> p t n", p=P)
                sp.wait_ge(s["branch"], KD)
                sp.dma_start(k.wring[:, 0, :].rearrange("p (t n) -> p t n", t=KD), w_o[:, :, 512:D]).then_inc(s_w[3], 16)

            @block.tensor
            def _(pe):
                pe.wait_ge(s_w[0], 16)
                pe.wait_ge(s_w[1], 16)
                for d in range(KD):
                    if d >= 2:
                        pe.wait_ge(s["dve"], 2 * (d - 1))
                    for br, z0 in ((0, 0), (1, Z_B)):
                        w = k.wring[:, br, :].rearrange("p (t n) -> p t n", t=4)
                        for t in range(4):
                            for hf in range(2):
                                mm = nc.tensor.matmul(ps[:, 4 * (d % 2) + 2 * br + hf, 0:HALF], w[:, t, d * P:(d + 1) * P],
                                                      k.zT[:, z0 + t, hf * HALF:(hf + 1) * HALF],
                                                      start=(t == 0), stop=(t == 3))
                    mm.then_inc(s["branch"], 1)
                pe.wait_ge(s["merged"], KD)
                for d in range(KD):
                    if d == 0:
                        pe.wait_ge(s_w[2], 16)
                    if d == 4:
                        pe.wait_ge(s_w[3], 16)
                    if d >= 4:
                        pe.wait_ge(s["gated_act"], d - 3)
                        pe.wait_ge(s["gated_dve"], 2 * (d - 3))
                    w = k.wring[:, 2 if d < 4 else 0, :].rearrange("p (t n) -> p t n", t=KD)
                    for t in range(KD):
                        for hf in range(2):
                            mm = nc.tensor.matmul(ps[:, 2 * (d % 4) + hf, 0:HALF], w[:, t, (d % 4) * P:(d % 4 + 1) * P],
                                                  mT[:, t, hf * HALF:(hf + 1) * HALF], start=(t == 0), stop=(t == KD - 1))
                    mm.then_inc(s["mix"], 1)
                pe.wait_ge(s["gated_act"], KD)
                pe.wait_ge(s["gated_dve"], 2 * KD)
                for i, (t0, w) in enumerate(TT):
                    if i == 4:
                        pe.wait_ge(s["x1"], 1)
                    for d in range(KD):
                        mm = nc.tensor.transpose(ps[0:w, 2 * (i % 4) + d // 4, (d % 4) * P:(d % 4 + 1) * P],
                                                 gm[:, d, t0:t0 + w], k.ident[:, :])
                    mm.then_inc(s["turned"], 1)

            @block.scalar
            def _(act):
                for d in range(KD):
                    for z0 in (Z_GA, Z_GC):
                        nc.scalar.activation(k.zT[:, z0 + d, :], k.zT[:, z0 + d, :], ACT.Sigmoid).then_inc(s["sig"], 1)
                for d in range(KD):
                    act.wait_ge(s["mix"], d + 1)
                    nc.scalar.mul(gm[:, d, 0:HALF], ps[:, 2 * (d % 4), 0:HALF], k.mod[:, 16 + d, 0:1]).then_inc(s["gated_act"], 1)

            @block.vector
            def _(dve):
                for d in range(KD):
                    dve.wait_ge(s["branch"], d + 1)
                    dve.wait_ge(s["sig"], 2 * (d + 1))
                    b = 4 * (d % 2)
                    nc.vector.tensor_tensor(halves(mT[:, d, :]), ps[:, b:b + 2, 0:HALF], halves(k.zT[:, Z_GA + d, :]),
                                            ALU.mult).then_inc(s["dve"], 1)
                    if d:
                        dve.wait_ge(s["merged"], d)
                    nc.vector.tensor_tensor(halves(tmp[:, :]), ps[:, b + 2:b + 4, 0:HALF], halves(k.zT[:, Z_GC + d, :]),
                                            ALU.mult).then_inc(s["dve"], 1)
                    dve.wait_ge(s["dve"], 2 * (d + 1))
                    nc.vector.tensor_tensor(mT[:, d, :], mT[:, d, :], tmp[:, :], ALU.add).then_inc(s["merged"], 1)
                for d in range(KD):
                    dve.wait_ge(s["mix"], d + 1)
                    for g, (a, b) in enumerate(((HALF, TP), (TP, T))):
                        nc.vector.tensor_scalar(gm[:, d, a:b], ps[:, 2 * (d % 4) + 1, a - HALF:b - HALF],
                                                k.mod[:, 16 + d, g:g + 1], None, ALU.mult).then_inc(s["gated_dve"], 1)
                for i, (t0, w) in enumerate(TT):
                    dve.wait_ge(s["turned"], i + 1)
                    b = 2 * (i % 4)
                    xv = k.x[0:w, i, :].rearrange("p (h c) -> p h c", h=2)
                    nc.vector.tensor_tensor(xv, xv, ps[0:w, b:b + 2, :], ALU.add).then_inc(s["x1"], 1)


def norm2_phase(nc, k, sem):
    names = ("sq", "mean", "inv", "root", "xn", "turned", "h_dve", "h_act", "hi", "lo", "zero")
    s = {n: sem("n2_" + n) for n in names}
    with ExitStack() as ctx:
        sq = ctx.enter_context(nc.sbuf_tensor("sq2", [P, D], F32))
        xn = ctx.enter_context(nc.sbuf_tensor("xn2", [P, 2, D], F32))
        st = ctx.enter_context(nc.sbuf_tensor("st2", [P, 4, 8], F32))
        psT = ctx.enter_context(nc.psum_tensor("psT2", [P, 2, KD, P], F32))
        with nc.Block() as block:
            @block.sync
            def _(sp):
                sp.dma_start(k.wpq[:, :, :], k.w_pq[0].rearrange("(t p) n -> p t n", p=P)).then_inc(k.s_wpq, 16)
                for n, src in enumerate((k.sub_keys1, k.sub_keys2)):
                    sp.dma_start(k.subk[:, :, n, :], src[0].rearrange("h q d -> q h d")).then_inc(k.s_subk, 16)

            @block.tensor
            def _(pe):
                for i, (t0, w) in enumerate(TT):
                    pe.wait_ge(s["xn"], i + 1)
                    if i >= 2:
                        pe.wait_ge(s["h_dve"], 4 * (i - 1))
                        pe.wait_ge(s["h_act"], 4 * (i - 1))
                    for t in range(KD):
                        mm = nc.tensor.transpose(psT[:, i % 2, t, 0:w], xn[0:w, i % 2, t * P:(t + 1) * P],
                                                 k.ident[0:w, 0:w])
                    mm.then_inc(s["turned"], 1)

            @block.scalar
            def _(act):
                for i, (t0, w) in enumerate(TT):
                    if i:
                        act.wait_ge(s["sq"], i)
                    nc.scalar.activation(sq[0:w, :], k.x[0:w, i, :], ACT.Square,
                                         accum_out=st[0:w, 0, i:i + 1]).then_inc(s["sq"], 1)
                for i, (t0, w) in enumerate(TT):
                    act.wait_ge(s["inv"], i + 1)
                    nc.scalar.activation(st[0:w, 3, i:i + 1], st[0:w, 2, i:i + 1], ACT.Sqrt).then_inc(s["root"], 1)
                act.wait_ge(s["zero"], 3)
                for i, (t0, w) in enumerate(TT):
                    g = i // 4
                    act.wait_ge(s["turned"], i + 1)
                    for t in range(KD // 2, KD):
                        nc.scalar.activation(k.h2T[:, t, t0:t0 + w], psT[:, i % 2, t, 0:w], ACT.Identity,
                                             bias=k.mod[:, 24 + t, g:g + 1], scale=k.fac[:, 1, t, g:g + 1]).then_inc(s["h_act"], 1)
                    act.wait_ge(s["h_dve"], 4 * (i + 1))
                    act.wait_ge(s["h_act"], 4 * (i + 1))
                    nc.scalar.copy(k.h2hi[:, :, t0:t0 + w], k.h2T[:, :, t0:t0 + w]).then_inc(s["hi"], 1)

            @block.vector
            def _(dve):
                nc.vector.memset(k.h2T[:, :, T:TPAD], 0.0).then_inc(s["zero"], 1)
                nc.vector.tensor_scalar(k.fac[:, 1, :, :], k.mod[:, 32:40, :], 1.0, None, ALU.add).then_inc(s["zero"], 1)
                dve.wait_ge(s["zero"], 2)
                nc.vector.tensor_tensor(k.fac[:, 1, :, :], k.fac[:, 1, :, :],
                                        bc(k.vT[:, C_G2:C_G2 + 8], 2, 2), ALU.mult).then_inc(s["zero"], 1)
                dve.wait_ge(s["zero"], 3)
                for i, (t0, w) in enumerate(TT):
                    dve.wait_ge(s["sq"], i + 1)
                    nc.vector.tensor_scalar(st[0:w, 1, i:i + 1], st[0:w, 0, i:i + 1], 1.0 / D, EPS,
                                            ALU.mult, ALU.add).then_inc(s["mean"], 1)
                    dve.wait_ge(s["mean"], i + 1)
                    nc.vector.reciprocal(st[0:w, 2, i:i + 1], st[0:w, 1, i:i + 1]).then_inc(s["inv"], 1)

                def scale(i):
                    w = TT[i][1]
                    dve.wait_ge(s["root"], i + 1)
                    nc.vector.tensor_scalar(xn[0:w, i % 2, :], k.x[0:w, i, :], st[0:w, 3, i:i + 1], None,
                                            ALU.mult).then_inc(s["xn"], 1)
                scale(0)
                scale(1)
                for i, (t0, w) in enumerate(TT):
                    g = i // 4
                    dve.wait_ge(s["turned"], i + 1)
                    if i + 2 < NTT:
                        scale(i + 2)
                    for t in range(KD // 2):
                        nc.vector.tensor_scalar(k.h2T[:, t, t0:t0 + w], psT[:, i % 2, t, 0:w], k.fac[:, 1, t, g:g + 1],
                                                k.mod[:, 24 + t, g:g + 1], ALU.mult, ALU.add).then_inc(s["h_dve"], 1)
                    dve.wait_ge(s["hi"], i + 1)
                    nc.vector.tensor_tensor(k.h2lo[:, :, t0:t0 + w], k.h2T[:, :, t0:t0 + w], k.h2hi[:, :, t0:t0 + w],
                                            ALU.subtract).then_inc(s["lo"], 1)


def experts_phase(nc, k, sem):
    names = ("keys", "keysT", "q_ps", "q_sb", "s_ps", "s_sb", "best", "dve", "shifted", "exp", "rows", "rows_turned",
             "pairs", "iota", "staged", "hot", "weighted", "made", "evicted", "turned", "hi", "lo", "up", "gelu")
    s = {n: sem("ex_" + n) for n in names}
    s_u = [sem(f"ex_u{i}") for i in range(2)]
    s_a = [sem(f"ex_a{i}") for i in range(2)]
    s_g = [sem(f"ex_g{i}") for i in range(2)]
    M = 2 * PH
    NK = PH * TOPK
    NE = NEXP // P
    NTOP, NGATE, NREST = 8, 4, 4
    TOP0, GATE0 = 0, NTOP * NTT
    REST0 = GATE0 + NGATE * (NGB // 2)
    NG = GTOK // 4
    HOT = 8
    NS = NTT + 1
    NDVE = 5 * M + 2 + 5 * PH + 3 + 1 + 6 + 3
    with ExitStack() as ctx:
        def sb(name, shape, dt=F32):
            return ctx.enter_context(nc.sbuf_tensor(name, shape, dt))
        skT = sb("skT", [P, M, NKEY])
        qT = sb("qT", [P, M, P])
        sc = sb("sc2", [P, M, NKEY])
        left = sb("left", [P, M, NKEY])
        cand = k.cand
        eq = left[:, :, :].rearrange("p m c -> p (m c)").rearrange("p (n a) -> p n a", a=TOPK)
        val = sb("val", [P, M, TOPK])
        idx = sb("idx", [P, M, TOPK], U32)
        idxf = sb("idxf", [P, M, TOPK])
        top = sb("top", [P, PH, TOPK])
        pos = sb("pos", [P, PH, TOPK], U32)
        posu = sb("posu", [P, 2, PH, TOPK], U32)
        posf = sb("posf", [P, 2, PH, TOPK])
        rows = sb("rows", [P, 3, NK])
        esum = sb("esum", [P, 2, PH])
        ghi = sb("ghi", [P, P], BF16)
        iota16 = sb("iota16", [P, TOPK])
        carrier = sb("carrier", [P, 1])
        uraw = sb("uraw", [P, 2, D])
        uhi = sb("uhi", [P, 2, KD, P], BF16)
        ulo = sb("ulo", [P, 2, KD, P], BF16)
        aout = sb("aout", [P, 2, T])
        gst = k.wpq[:, 0:4, :].rearrange("p a n -> p (a n)").rearrange("p (b i t) -> p b i t", b=2, t=GTOK)
        hot = k.wpq[:, 4:7, :].rearrange("p a n -> p (a n)").bitcast(BF16)[:, 0:HOT * 4 * 3 * P].rearrange(
            "p (s c f i) -> p s c f i", s=HOT, c=4, f=3)
        stg = k.wpq[:, 7, 0:2 * 4 * GTOK].rearrange("p (b f t) -> p b f t", b=2, f=4)
        psA = ctx.enter_context(nc.psum_tensor("psA", [P, 2, 512], F32))
        psT = ctx.enter_context(nc.psum_tensor("psT3", [P, KD, P], F32))
        psD = ctx.enter_context(nc.psum_tensor("psD", [P, 2, 2, 512], F32))
        quad = "p (c q) -> p c q"

        def tile(base, it, n, r):
            return it * n + (base + r)

        def half(base, it, n, r):
            return it * (n // 2) + (base // 2 + r // 2)

        with nc.Block() as block:
            @block.gpsimd
            def _(pool):
                nc.gpsimd.iota(iota16[:, :], [[1, TOPK]], base=0, channel_multiplier=0,
                               allow_small_or_imprecise_dtypes=True).then_inc(s["iota"], 1)
                pool.wait_ge(s["iota"], 1)
                nc.gpsimd.iota(k.iota128[:, :], [[1, P]], base=0, channel_multiplier=0,
                               allow_small_or_imprecise_dtypes=True).then_inc(s["iota"], 1)
                pool.wait_ge(s["iota"], 2)
                pool.sem_inc(s["weighted"], 4 * NG)
                with pool.Fori(0, NGB // 2) as it:
                    for u in range(2 * NG):
                        b = u // NG
                        if u % NG == 0:
                            pool.wait_ge(s["staged"], it * 2 + (b + NS + 1))
                        pool.wait_ge(s["hot"], it * (2 * NG) + (u + 1))
                        t = 4 * (u % NG)
                        second = hot[:, u % HOT, :, 2, :]
                        nc.gpsimd.tensor_tensor(hot[:, u % HOT, :, 1, :], second, bc(stg[:, b, 2, t:t + 4], 2, P),
                                                ALU.mult).then_inc(s["weighted"], 1)
                        pool.wait_ge(s["weighted"], it * (4 * NG) + (2 * u + 1 + 4 * NG))
                        nc.gpsimd.tensor_tensor(second, second, bc(stg[:, b, 3, t:t + 4], 2, P),
                                                ALU.mult).then_inc(s["weighted"], 1)

            @block.sync
            def _(sp):
                def load(it, r):
                    sp.dma_start(uraw[:, r:r + 1, :], k.expert_u[0].rearrange("(e p) d -> p e d", p=P)
                                 [:, ds(it * 2 + r, 1), :]).then_inc(s_u[r], 16)
                for r in range(2):
                    load(0, r)
                with sp.Fori(1, NE // 2) as it:
                    for r in range(2):
                        sp.wait_ge(s["turned"], it * 2 + (r - 1))
                        load(it, r)

            @block.tensor
            def _(pe):
                def turn(base, it, n, r):
                    e = tile(base, it, n, r)
                    pe.wait_ge(s_u[r % 2], half(base, it, n, r) * 16 + 16)
                    pe.wait_ge(s["lo"], e + 1)
                    for t in range(KD):
                        mm = nc.tensor.transpose(psT[:, t, :], uraw[:, r % 2, t * P:(t + 1) * P], k.ident[:, :])
                    mm.then_inc(s["turned"], 1)

                def up(base, it, n, r, between=None):
                    e = tile(base, it, n, r)
                    pe.wait_ge(s["lo"], e + 2)
                    pe.wait_ge(s["gelu"], e + 1)
                    q = r % 2
                    for t in range(KD):
                        for w, hs in ((uhi, (k.h2hi, k.h2lo)), (ulo, (k.h2hi,))):
                            for m, hx in enumerate(hs):
                                for hf in range(2):
                                    mm = nc.tensor.matmul(psD[:, q, hf, 0:HALF], w[:, q, t, :],
                                                          hx[:, t, hf * HALF:(hf + 1) * HALF],
                                                          start=(t == 0 and w is uhi and m == 0),
                                                          stop=(t == KD - 1 and w is ulo))
                        if between is not None and t in (0, 2, 4, 6):
                            between(t // 2)
                    mm.then_inc(s["up"], 1)

                def queries(it, j):
                    pe.wait_ge(s["q_sb"], it * 4 + (j + 1))
                    for c in range(4):
                        m = 4 * j + c
                        for t in range(KD):
                            mm = nc.tensor.matmul(psA[:, 0, c * P:(c + 1) * P], k.wpq[:, t, m * P:(m + 1) * P],
                                                  k.h2T[:, t, ds(it * P, P)], start=(t == 0), stop=(t == KD - 1))
                    mm.then_inc(s["q_ps"], 1)

                def scores(it, j):
                    pe.wait_ge(s["q_sb"], it * 4 + (j + 2))
                    pe.wait_ge(s["s_sb"], it * 4 + (j + 1))
                    for c in range(4):
                        m = 4 * j + c
                        mm = nc.tensor.matmul(psA[:, 1, c * P:(c + 1) * P], qT[:, m, :], skT[:, m, :],
                                              start=True, stop=True)
                    mm.then_inc(s["s_ps"], 1)

                def turn_rows(it, final=False):
                    pe.wait_ge(s["rows"], it + 1)
                    if final:
                        pe.wait_ge(s["pairs"], it)
                    else:
                        pe.wait_ge(s["s_sb"], it * 4 + 5)
                    for f in range(3):
                        mm = nc.tensor.transpose(psA[:, 1, f * P:(f + 1) * P], rows[:, f, :], k.ident[:, :])
                    mm.then_inc(s["rows_turned"], 1)

                def retrieval_pass(it, following):
                    for r in range(NTOP):
                        turn(TOP0, it, NTOP, r + 1)
                        if following and r < 4:
                            queries(it + 1, r)
                        if r == 1:
                            turn_rows(it)
                        if following and r >= 4:
                            if r == 4:
                                pe.wait_ge(s["pairs"], it + 1)
                            scores(it + 1, r - 4)
                        up(TOP0, it, NTOP, r)

                def gate_group(it, u):
                    pe.wait_ge(s["weighted"], it * (4 * NG) + (2 * u + 2 + 4 * NG))
                    pe.wait_ge(s["evicted"], it * (2 * NG) + (u + 1))
                    for c in range(4):
                        for f in range(2):
                            mm = nc.tensor.matmul(psA[:, u % 2, c * P:(c + 1) * P], hot[:, u % HOT, c, 1 + f, :],
                                                  hot[:, u % HOT, c, 0, :], start=(f == 0), stop=(f == 1))
                    mm.then_inc(s["made"], 1)

                pe.sem_inc(s["up"], 2)
                pe.sem_inc(s["made"], HOT)
                pe.wait_ge(k.s_subk, 32)
                for j in range(4):
                    if j:
                        pe.wait_ge(s["keysT"], j)
                    for c in range(4):
                        m = 4 * j + c
                        mm = nc.tensor.transpose(psA[:, 0, c * P:(c + 1) * P], k.subk[:, m // 2, m % 2, :], k.ident[:, :])
                    mm.then_inc(s["keys"], 1)
                pe.wait_ge(s["keysT"], 4)
                pe.wait_ge(k.s_wpq, 16)
                turn(TOP0, 0, NTOP, 0)
                for j in range(4):
                    queries(0, j)
                    scores(0, j)
                with pe.Fori(0, NTT - 1) as it:
                    retrieval_pass(it, True)
                retrieval_pass(NTT - 1, False)
                turn_rows(NTT, True)
                with pe.Fori(0, NGB // 2) as it:
                    for r in range(NGATE):
                        turn(GATE0, it, NGATE, r + 1)
                        up(GATE0, it, NGATE, r, lambda c: gate_group(it, 4 * r + c))
                NR = (NE - REST0) // NREST
                with pe.Fori(0, NR - 1) as it:
                    for r in range(NREST):
                        turn(REST0, it, NREST, r + 1)
                        up(REST0, it, NREST, r)
                for r in range(NREST):
                    if r < NREST - 1:
                        turn(REST0, NR - 1, NREST, r + 1)
                    up(REST0, NR - 1, NREST, r)

            @block.scalar
            def _(act):
                def high(base, it, n, r):
                    e = tile(base, it, n, r)
                    act.wait_ge(s["turned"], e + 1)
                    act.wait_ge(s["up"], e + 1)
                    nc.scalar.copy(uhi[:, r % 2, :, :], psT[:, :, :]).then_inc(s["hi"], 1)

                def gelu(base, it, n, r):
                    e = tile(base, it, n, r)
                    act.wait_ge(s["up"], e + 3)
                    act.wait_ge(s_a[r % 2], half(base, it, n, r) * 16 + 16)
                    nc.scalar.activation(aout[:, r % 2, :].rearrange("p (h c) -> p h c", h=2), psD[:, r % 2, :, 0:HALF],
                                         ACT.Gelu_apprx_tanh).then_inc(s["gelu"], 1)
                    act.wait_ge(s["gelu"], e + 3)
                    act.dma_start(k.act_dram[ds(e, 1)].rearrange("e p t -> p e t"),
                                  aout[:, r % 2:r % 2 + 1, :]).then_inc(s_a[r % 2], 16)

                def keep_queries(it, j):
                    act.wait_ge(s["q_ps"], it * 4 + (j + 1))
                    if j == 0:
                        act.wait_ge(s["s_ps"], it * 4)
                    nc.scalar.copy(qT[:, 4 * j:4 * j + 4, :], psA[:, 0, :].rearrange(quad, c=4)).then_inc(s["q_sb"], 1)

                def keep_scores(it, j):
                    act.wait_ge(s["s_ps"], it * 4 + (j + 1))
                    if j == 0:
                        act.wait_ge(s["best"], it)
                    nc.scalar.copy(sc[:, 4 * j:4 * j + 4, :], psA[:, 1, :].rearrange(quad, c=4)).then_inc(s["s_sb"], 1)

                def retrieval_pass(it, following):
                    for r in range(NTOP):
                        high(TOP0, it, NTOP, r + 1)
                        if following and r < 4:
                            keep_queries(it + 1, r)
                        if following and r >= 4:
                            keep_scores(it + 1, r - 4)
                        if r == 6:
                            act.wait_ge(s["shifted"], it + 1)
                            nc.scalar.activation(top[:, :, :], top[:, :, :], ACT.Exp).then_inc(s["exp"], 1)
                        gelu(TOP0, it, NTOP, r)

                act.sem_inc(s["gelu"], 2)
                act.sem_inc(s["q_sb"], 1)
                act.sem_inc(s["s_sb"], 1)
                act.sem_inc(s["evicted"], 2)
                for q in range(2):
                    act.sem_inc(s_a[q], 16)
                    act.sem_inc(s_g[q], 16)
                for j in range(4):
                    act.wait_ge(s["keys"], j + 1)
                    nc.scalar.copy(skT[:, 4 * j:4 * j + 4, :], psA[:, 0, :].rearrange(quad, c=4)).then_inc(s["keysT"], 1)
                high(TOP0, 0, NTOP, 0)
                for j in range(4):
                    act.wait_ge(s["q_ps"], j + 1)
                    nc.scalar.copy(qT[:, 4 * j:4 * j + 4, :], psA[:, 0, :].rearrange(quad, c=4)).then_inc(s["q_sb"], 1)
                    act.wait_ge(s["s_ps"], j + 1)
                    nc.scalar.copy(sc[:, 4 * j:4 * j + 4, :], psA[:, 1, :].rearrange(quad, c=4)).then_inc(s["s_sb"], 1)
                with act.Fori(0, NTT - 1) as it:
                    retrieval_pass(it, True)
                retrieval_pass(NTT - 1, False)
                with act.Fori(0, NGB // 2) as it:
                    for r in range(NGATE):
                        high(GATE0, it, NGATE, r + 1)
                        b = r // 2
                        if r % 2 == 0:
                            act.wait_ge(s_g[b], it * 16 + 16)
                        for c in range(4):
                            u = 4 * r + c
                            act.wait_ge(s["made"], it * (2 * NG) + (u + 1 + HOT))
                            g = u % NG
                            nc.scalar.copy(gst[:, b, :, 4 * g:4 * g + 4].rearrange("p i t -> p t i"),
                                           psA[:, u % 2, :].rearrange("p (t i) -> p t i", t=4)).then_inc(s["evicted"], 1)
                        if r % 2 == 1:
                            act.wait_ge(s["evicted"], it * (2 * NG) + (4 * r + 6))
                            act.dma_start(k.gate_dram[ds(it * 2 + b, 1)].rearrange("b p i t -> p b (i t)"),
                                          gst[:, b:b + 1, :, :].rearrange("p b i t -> p b (i t)")).then_inc(s_g[b], 16)
                        gelu(GATE0, it, NGATE, r)
                NR = (NE - REST0) // NREST
                with act.Fori(0, NR - 1) as it:
                    for r in range(NREST):
                        high(REST0, it, NREST, r + 1)
                        gelu(REST0, it, NREST, r)
                for r in range(NREST):
                    if r < NREST - 1:
                        high(REST0, NR - 1, NREST, r + 1)
                    gelu(REST0, NR - 1, NREST, r)
                for q in range(2):
                    act.wait_ge(s_a[q], 16 * (NE // 2 + 1))
                    act.wait_ge(s_g[q], 16 * (NGB // 2 + 1))

            @block.vector
            def _(dve):
                def low(base, it, n, r):
                    dve.wait_ge(s["hi"], tile(base, it, n, r) + 1)
                    nc.vector.tensor_tensor(ulo[:, r % 2, :, :], psT[:, :, :], uhi[:, r % 2, :, :],
                                            ALU.subtract).then_inc(s["lo"], 1)

                def retrieval_pass(it):
                    n = Chain(s["dve"], it, NDVE)

                    def settle():
                        dve.wait_ge(s["dve"], n.at())

                    def stand():
                        nc.vector.memset(carrier[:, :], 0.0)

                    def first8(src, v, count):
                        for m in range(count):
                            n.did(nc.vector.max(v[:, m, 0:8], src[:, m, :]))

                    def places8(src, rest, v, ix, count):
                        settle()
                        stand()
                        for m in range(count):
                            n.did(nc.vector.max_index(ix[:, m, 0:8], v[:, m, 0:8], src[:, m, :]))
                            n.did(nc.vector.match_replace(rest[:, m, :], v[:, m, 0:8], src[:, m, :], -3.0e38))

                    def next8(rest, v, ix, count):
                        settle()
                        stand()
                        for m in range(count):
                            n.did(nc.vector.max(v[:, m, 8:16], rest[:, m, :]))
                        settle()
                        stand()
                        for m in range(count):
                            n.did(nc.vector.max_index(ix[:, m, 8:16], v[:, m, 8:16], rest[:, m, :]))

                    def choose(side):
                        fi = idxf[:, :, :].rearrange("p (h n) a -> p h n a", n=2)
                        e4 = eq.rearrange("p (h k) a -> p h k a", h=PH)
                        settle()
                        n.did(nc.vector.tensor_tensor(eq, bc(posf[:, side, :, :].rearrange("p h k -> p (h k)"), 2, TOPK),
                                                      bc(iota16[:, :], 1, NK), ALU.is_equal))
                        settle()
                        n.did(nc.vector.tensor_tensor(e4, e4, bc(fi[:, :, side, :], 2, TOPK), ALU.mult))
                        settle()
                        n.did(nc.vector.tensor_reduce(rows[:, side, :], eq, AX_X, ALU.add))

                    low(TOP0, it, NTOP, 1)
                    dve.wait_ge(s["s_sb"], it * 4 + 5)
                    stand()
                    first8(sc, val, M)
                    low(TOP0, it, NTOP, 2)
                    places8(sc, left, val, idx, M)
                    low(TOP0, it, NTOP, 3)
                    next8(left, val, idx, M)
                    settle()
                    dve.sem_inc(s["best"], 1)
                    low(TOP0, it, NTOP, 4)
                    store_pairs(it)
                    n.did(nc.vector.tensor_copy(idxf[:, :, :], idx[:, :, :]))
                    v = val[:, :, :].rearrange("p (h n) a -> p h n a", n=2)
                    n.did(nc.vector.tensor_tensor(cand[:, :, :].rearrange("p h (a b) -> p h a b", a=TOPK),
                                                  bc(v[:, :, 0, :], 3, TOPK), bc(v[:, :, 1, :], 2, TOPK), ALU.add))
                    settle()
                    stand()
                    first8(cand, top, PH)
                    low(TOP0, it, NTOP, 5)
                    cleft = left[:, :, :].rearrange("p (h n) c -> p h (n c)", n=2)
                    places8(cand, cleft, top, pos, PH)
                    low(TOP0, it, NTOP, 6)
                    next8(cleft, top, pos, PH)
                    settle()
                    n.did(nc.vector.tensor_scalar(posu[:, 0, :, :], pos[:, :, :], 4, None, ALU.logical_shift_right))
                    n.did(nc.vector.tensor_scalar(posu[:, 1, :, :], pos[:, :, :], 15, None, ALU.bitwise_and))
                    n.did(nc.vector.tensor_copy(esum[:, 0, :], top[:, :, 0]))
                    settle()
                    n.did(nc.vector.tensor_copy(posf[:, :, :, :], posu[:, :, :, :]))
                    nc.vector.tensor_tensor(top[:, :, :], top[:, :, :], bc(esum[:, 0, :], 2, TOPK),
                                            ALU.subtract).then_inc(s["shifted"], 1)
                    low(TOP0, it, NTOP, 7)
                    choose(0)
                    low(TOP0, it, NTOP, 8)
                    choose(1)
                    dve.wait_ge(s["exp"], it + 1)
                    n.did(nc.vector.tensor_reduce(esum[:, 0, :], top[:, :, :], AX_X, ALU.add))
                    settle()
                    n.did(nc.vector.reciprocal(esum[:, 1, :], esum[:, 0, :]))
                    settle()
                    n.did(nc.vector.tensor_tensor(rows[:, 2, :].rearrange("p (h k) -> p h k", h=PH), top[:, :, :],
                                                  bc(esum[:, 1, :], 2, TOPK), ALU.mult))
                    settle()
                    dve.sem_inc(s["rows"], 1)
                    n.end()

                def store_pairs(it):
                    turned = psA[:, 1, 0:3 * P].rearrange("p (f t) -> p f t", f=3)
                    dve.wait_ge(s["rows_turned"], it + 1)
                    nc.vector.tensor_copy(ghi[:, :], turned[:, 2, :]).then_inc(s["staged"], 1)
                    nc.vector.tensor_scalar(k.pairs[:, 0:2, ds(it * P, P)], turned[:, 0:2, :], 1.0, None, ALU.mult)
                    dve.wait_ge(s["staged"], it + 1)
                    nc.vector.tensor_scalar(k.pairs[:, 2:3, ds(it * P, P)], ghi[:, :].unsqueeze(1), 1.0, None, ALU.mult)
                    nc.vector.tensor_tensor(k.pairs[:, 3:4, ds(it * P, P)], turned[:, 2:3, :], ghi[:, :].unsqueeze(1),
                                            ALU.subtract).then_inc(s["pairs"], 1)

                dve.sem_inc(s["lo"], 1)
                nc.vector.memset(rows[:, :, :], 0.0).then_inc(s["rows"], 1)
                dve.wait_ge(s["iota"], 2)
                low(TOP0, 0, NTOP, 0)
                with dve.Fori(0, NTT) as it:
                    retrieval_pass(it)
                store_pairs(NTT)
                dve.wait_ge(s["pairs"], NTT + 1)

                def stage(it, b):
                    dve.wait_ge(s["weighted"], it * (4 * NG) + (b + 1) * 2 * NG)
                    nc.vector.tensor_scalar(stg[:, b, :, :], k.pairs[:, :, ds(it * (2 * GTOK) + (P + b * GTOK), GTOK)],
                                            1.0, None, ALU.mult).then_inc(s["staged"], 1)
                    dve.wait_ge(s["staged"], it * 2 + (b + NS + 1))

                def one_hots(it, r):
                    b = r // 2
                    if r % 2 == 0:
                        stage(it, b)
                    for c4 in range(4):
                        u = 4 * r + c4
                        dve.wait_ge(s["made"], it * (2 * NG) + (u + 1))
                        t = 4 * (u % NG)
                        for key, plane in ((0, 0), (1, 2)):
                            ins = nc.vector.tensor_tensor(hot[:, u % HOT, :, plane, :], bc(k.iota128[:, :], 1, 4),
                                                          bc(stg[:, b, key, t:t + 4], 2, P), ALU.is_equal)
                        ins.then_inc(s["hot"], 1)

                one_hots(0, 0)
                with dve.Fori(0, NGB // 2 - 1) as it:
                    for r in range(NGATE):
                        low(GATE0, it, NGATE, r + 1)
                        if r < NGATE - 1:
                            one_hots(it, r + 1)
                        else:
                            one_hots(it + 1, 0)
                for r in range(NGATE):
                    low(GATE0, NGB // 2 - 1, NGATE, r + 1)
                    if r < NGATE - 1:
                        one_hots(NGB // 2 - 1, r + 1)
                NR = (NE - REST0) // NREST
                with dve.Fori(0, NR - 1) as it:
                    for r in range(NREST):
                        low(REST0, it, NREST, r + 1)
                for r in range(NREST - 1):
                    low(REST0, NR - 1, NREST, r + 1)


def down_phase(nc, k, sem):
    names = ("v_hi", "v_lo", "w", "w_hi", "w_lo", "down", "sum", "zero")
    s = {n: sem("dn_" + n) for n in names}
    s_v = [sem(f"dn_v{i}") for i in range(4)]
    s_a = [sem(f"dn_a{i}") for i in range(4)]
    s_g = [sem(f"dn_g{i}") for i in range(2)]
    NGR = NEXP // P // EG
    with ExitStack() as ctx:
        def sb(name, shape, dt=F32):
            return ctx.enter_context(nc.sbuf_tensor(name, shape, dt))
        vraw = sb("vraw", [P, 4, D])
        abuf = sb("abuf", [P, 4, T])
        gbuf = sb("gbuf", [P, 2, NGB, 4 * GTOK])
        wf = sb("wf", [P, 2, T])
        vh = sb("vh", [P, 2, EG, D], BF16)
        vl = sb("vl", [P, 2, EG, D], BF16)
        wh = sb("wh", [P, 2, EG, T], BF16)
        wl = sb("wl", [P, 2, EG, T], BF16)
        psY = ctx.enter_context(nc.psum_tensor("psY", [P, 4, 2, 512], F32))

        with nc.Block() as block:
            @block.sync
            def _(sp):
                def load(it, b, e, first=False):
                    n = it * 2 * EG + b * EG + e
                    if e % 4 == 0:
                        hf = e // 4
                        if not first:
                            sp.wait_ge(s["w"], n - 4)
                        sp.dma_start(gbuf[:, hf, :, :], k.gate_dram.rearrange("b p i t -> p b (i t)")
                                     [:, :, ds(n * GTOK, 4 * GTOK)]).then_inc(s_g[hf], 16)
                    if not (first and e < 4):
                        sp.wait_ge(s["w"], n - 3)
                    sp.dma_start(abuf[:, e % 4:e % 4 + 1, :], k.act_dram.rearrange("e p t -> p e t")
                                 [:, ds(n, 1), :]).then_inc(s_a[e % 4], 16)
                    if not (first and e < 4):
                        sp.wait_ge(s["v_lo"], n - 3)
                    sp.dma_start(vraw[:, e % 4:e % 4 + 1, :], k.expert_v[0].rearrange("(e p) d -> p e d", p=P)
                                 [:, ds(n, 1), :]).then_inc(s_v[e % 4], 16)
                for e in range(EG):
                    load(0, 0, e, True)
                for e in range(EG):
                    load(0, 1, e)
                with sp.Fori(1, NGR // 2) as it:
                    for b in range(2):
                        for e in range(EG):
                            load(it, b, e)

            @block.scalar
            def _(act):
                def split(it, b, e):
                    n = it * 2 * EG + b * EG + e
                    act.wait_ge(s_v[e % 4], (it * 4 + b * 2 + e // 4 + 1) * 16)
                    if e == 0:
                        act.wait_ge(s["down"], it * 2 * KD + b * KD + 1)
                    nc.scalar.copy(vh[:, b, e, :], vraw[:, e % 4, :]).then_inc(s["v_hi"], 1)
                    act.wait_ge(s["w"], n + 1)
                    nc.scalar.copy(wh[:, b, e, :], wf[:, e % 2, :]).then_inc(s["w_hi"], 1)
                with act.Fori(0, NGR // 2) as it:
                    for b in range(2):
                        for e in range(EG):
                            split(it, b, e)

            @block.vector
            def _(dve):
                def weigh(it, b, e):
                    n = it * 2 * EG + b * EG + e
                    dve.wait_ge(s_a[e % 4], (it * 4 + b * 2 + e // 4 + 1) * 16)
                    if e % 4 == 0:
                        dve.wait_ge(s_g[e // 4], (it * 2 + b + 1) * 16)
                    if e == 0:
                        dve.wait_ge(s["down"], it * 2 * KD + b * KD + 1)
                    tok = "p (b t) -> p b t"
                    nc.vector.tensor_tensor(wf[:, e % 2, :].rearrange(tok, t=GTOK), abuf[:, e % 4, :].rearrange(tok, t=GTOK),
                                            gbuf[:, e // 4, :, (e % 4) * GTOK:(e % 4 + 1) * GTOK], ALU.mult).then_inc(s["w"], 1)
                    dve.wait_ge(s["v_hi"], n + 1)
                    nc.vector.tensor_tensor(vl[:, b, e, :], vraw[:, e % 4, :], vh[:, b, e, :], ALU.subtract).then_inc(s["v_lo"], 1)
                    dve.wait_ge(s["w_hi"], n + 1)
                    nc.vector.tensor_tensor(wl[:, b, e, :], wf[:, e % 2, :], wh[:, b, e, :], ALU.subtract).then_inc(s["w_lo"], 1)

                def add(it, b, d):
                    n = it * 2 * KD + b * KD + d
                    dve.wait_ge(s["down"], n + KD + 1)
                    dve.wait_ge(s["sum"], n + 1)
                    y = k.acc[:, d, :].rearrange("p (h c) -> p h c", h=2)
                    nc.vector.tensor_tensor(y, y, psY[:, d % 4, :, 0:HALF], ALU.add).then_inc(s["sum"], 1)

                nc.vector.memset(k.acc[:, :, :], 0.0).then_inc(s["zero"], 1)
                dve.wait_ge(s["zero"], 1)
                dve.sem_inc(s["sum"], 4)
                for e in range(EG):
                    weigh(0, 0, e)
                with dve.Fori(0, NGR // 2 - 1) as it:
                    for b in range(2):
                        for e in range(EG):
                            weigh(it if b == 0 else it + 1, 1 - b, e)
                            add(it, b, e)
                last = NGR // 2 - 1
                for e in range(EG):
                    weigh(last, 1, e)
                    add(last, 0, e)
                for e in range(EG):
                    add(last, 1, e)
                dve.wait_ge(s["sum"], NGR * KD + 4)

            @block.tensor
            def _(pe):
                pe.sem_inc(s["down"], KD)
                with pe.Fori(0, NGR // 2) as it:
                    for b in range(2):
                        pe.wait_ge(s["v_lo"], it * 2 * EG + b * EG + EG)
                        pe.wait_ge(s["w_lo"], it * 2 * EG + b * EG + EG)
                        for d in range(KD):
                            n = it * 2 * KD + b * KD + d
                            pe.wait_ge(s["sum"], n + 1)
                            for e in range(EG):
                                for v, ws in ((vh, (wh, wl)), (vl, (wh,))):
                                    for m, w in enumerate(ws):
                                        for hf in range(2):
                                            mm = nc.tensor.matmul(psY[:, d % 4, hf, 0:HALF], v[:, b, e, d * P:(d + 1) * P],
                                                                  w[:, b, e, hf * HALF:(hf + 1) * HALF],
                                                                  start=(e == 0 and v is vh and m == 0),
                                                                  stop=(e == EG - 1 and v is vl))
                            mm.then_inc(s["down"], 1)


def output_phase(nc, k, sem):
    names = ("scaled", "turned", "added", "stored")
    s = {n: sem("out_" + n) for n in names}
    with ExitStack() as ctx:
        ps = ctx.enter_context(nc.psum_tensor("psOut", [P, 4, 2, 512], F32))
        with nc.Block() as block:
            @block.vector
            def _(dve):
                for d in range(KD):
                    for g, (g0, gw) in enumerate(GROUP_COLS):
                        nc.vector.tensor_scalar(k.acc[:, d, g0:g0 + gw], k.acc[:, d, g0:g0 + gw],
                                                k.mod[:, 40 + d, g:g + 1], None, ALU.mult).then_inc(s["scaled"], 1)
                for i, (t0, w) in enumerate(TT):
                    dve.wait_ge(s["turned"], i + 1)
                    xv = k.x[0:w, i, :].rearrange("p (h c) -> p h c", h=2)
                    nc.vector.tensor_tensor(xv, xv, ps[0:w, i % 4, :, :], ALU.add).then_inc(s["added"], 1)

            @block.tensor
            def _(pe):
                pe.wait_ge(s["scaled"], 2 * KD)
                for i, (t0, w) in enumerate(TT):
                    if i == 4:
                        pe.wait_ge(s["added"], 1)
                    for d in range(KD):
                        mm = nc.tensor.transpose(ps[0:w, i % 4, d // 4, (d % 4) * P:(d % 4 + 1) * P],
                                                 k.acc[:, d, t0:t0 + w], k.ident[:, :])
                    mm.then_inc(s["turned"], 1)

            @block.sync
            def _(sp):
                for i, (t0, w) in enumerate(TT):
                    sp.wait_ge(s["added"], i + 1)
                    dst = k.o_y_p[0, t0:t0 + w, :] if i < 4 else k.o_y_s[0]
                    sp.dma_start(dst, k.x[0:w, i, :]).then_inc(s["stored"], 16)
                sp.wait_ge(s["stored"], 16 * NTT)


_INS = ['x_prompt', 'c_prompt', 'x_sample', 'c_sample', 'cache_k', 'cache_v', 'cache_conv', 'w_ada', 'b_ada',
        'norm1_gain', 'norm2_gain', 'w_in', 'q_gain', 'k_gain', 'rel_table', 'conv_w', 'w_o_att', 'w_o_conv',
        'w_o', 'w_pq', 'sub_keys1', 'sub_keys2', 'expert_u', 'expert_v']


_OUTS = [("o_y_p", (1, 512, 1024)), ("o_y_s", (1, 64, 1024)),
         ("o_k_p", (1, 1, 512, 8, 64)), ("o_v_p", (1, 1, 512, 8, 64)), ("o_conv_p", (1, 1, 2, 512)),
         ("o_k_s", (1, 1, 64, 8, 64)), ("o_v_s", (1, 1, 64, 8, 64)), ("o_conv_s", (1, 1, 2, 512))]


def program(nc, ins, outs):
    k = Kernel()
    k.x_prompt = ins["x_prompt"]
    k.c_prompt = ins["c_prompt"]
    k.x_sample = ins["x_sample"]
    k.c_sample = ins["c_sample"]
    k.cache_k = ins["cache_k"]
    k.cache_v = ins["cache_v"]
    k.cache_conv = ins["cache_conv"]
    k.w_ada = ins["w_ada"]
    k.b_ada = ins["b_ada"]
    k.norm1_gain = ins["norm1_gain"]
    k.norm2_gain = ins["norm2_gain"]
    k.w_in = ins["w_in"]
    k.q_gain = ins["q_gain"]
    k.k_gain = ins["k_gain"]
    k.rel_table = ins["rel_table"]
    k.conv_w = ins["conv_w"]
    k.w_o_att = ins["w_o_att"]
    k.w_o_conv = ins["w_o_conv"]
    k.w_o = ins["w_o"]
    k.w_pq = ins["w_pq"]
    k.sub_keys1 = ins["sub_keys1"]
    k.sub_keys2 = ins["sub_keys2"]
    k.expert_u = ins["expert_u"]
    k.expert_v = ins["expert_v"]
    k.rel_ext = ins["rel_ext"]
    k.gate_dram = ins["gate_dram"]
    k.act_dram = ins["act_dram"]
    k.o_y_p = outs["o_y_p"]
    k.o_y_s = outs["o_y_s"]
    k.o_k_p = outs["o_k_p"]
    k.o_v_p = outs["o_v_p"]
    k.o_conv_p = outs["o_conv_p"]
    k.o_k_s = outs["o_k_s"]
    k.o_v_s = outs["o_v_s"]
    k.o_conv_s = outs["o_conv_s"]
    with ExitStack() as ctx:
        def sb(name, shape, dt=F32):
            return ctx.enter_context(nc.sbuf_tensor(name, shape, dt))

        def sem(name):
            return ctx.enter_context(nc.semaphore(name))
        k.x = sb("x", [P, NTT, D])
        k.ident = sb("ident", [P, P])
        k.flip = sb("flip", [P, P])
        k.blk64 = sb("blk64", [P, P])
        k.vT = sb("vT", [P, NVEC])
        k.siluc = sb("siluc", [P, KD, 2])
        k.mod = sb("mod", [P, 48, 2])
        k.fac = sb("fac", [P, 2, KD, 2])
        k.s_x = [sem(f"x_loaded{i}") for i in range(NTT)]
        k.s_ada = [sem(f"ada_loaded{i}") for i in range(4)]
        k.s_adr = [sem(f"ada_pass_loaded{i}") for i in range(2)]
        k.s_mg = [sem(f"merge_weights{i}") for i in range(4)]
        k.s_win = [sem(f"win_loaded{i}") for i in range(2)]
        with ExitStack() as front:
            k.zT = front.enter_context(nc.sbuf_tensor("zT", [P, 40, T], F32))
            k.wring = front.enter_context(nc.sbuf_tensor("wring", [P, 3, WBLK], F32))
            setup_phase(nc, k, sem)
            with ExitStack() as hs:
                k.hT = hs.enter_context(nc.sbuf_tensor("hT", [P, KD, T], F32))
                ada_phase(nc, k, sem)
                z_phase(nc, k, sem)
            with ExitStack() as att:
                k.bias = att.enter_context(nc.sbuf_tensor("bias", [P, NHEAD, 256], F32))
                k.kcT = att.enter_context(nc.sbuf_tensor("kcT", [P, 4, P], F32))
                k.cv = att.enter_context(nc.sbuf_tensor("cv", [P, ATT], F32))
                prep_phase(nc, k, sem)
                attention_phase(nc, k, sem)
            merge_phase(nc, k, sem)
        with ExitStack() as mid:
            def sbm(name, shape, dt=F32):
                return mid.enter_context(nc.sbuf_tensor(name, shape, dt))
            k.h2hi = sbm("h2hi", [P, KD, T], BF16)
            k.h2lo = sbm("h2lo", [P, KD, T], BF16)
            k.pairs = sbm("pairs", [P, 4, P + TPAD])
            k.iota128 = sbm("iota128", [P, P], BF16)
            with ExitStack() as tk:
                k.h2T = tk.enter_context(nc.sbuf_tensor("h2T", [P, KD, TPAD], F32))
                k.wpq = tk.enter_context(nc.sbuf_tensor("wpq", [P, KD, 2 * PH * P], F32))
                k.cand = tk.enter_context(nc.sbuf_tensor("cand", [P, PH, TOPK * TOPK], F32))
                k.subk = k.cand[:, :, :].rearrange("p h (n d) -> p h n d", n=2)
                k.s_wpq = sem("w_pq_loaded")
                k.s_subk = sem("sub_keys_loaded")
                norm2_phase(nc, k, sem)
                experts_phase(nc, k, sem)
        k.acc = sb("acc", [P, KD, T])
        down_phase(nc, k, sem)
        output_phase(nc, k, sem)


def kernel(**inputs):
    import numpy as _np
    import concourse.bacc as _bacc
    from concourse import mybir as _mybir
    from concourse.bass_utils import run_bass_kernel_spmd as _run
    nc = _bacc.Bacc("TRN2", target_bir_lowering=False, num_devices=1)
    arrays, ins = {}, {}
    for name in _INS:
        a = _np.ascontiguousarray(inputs[name])
        arrays[f"in_{name}_dram"] = a
        ins[name] = nc.dram_tensor(f"in_{name}_dram", a.shape, _mybir.dt.from_np(a.dtype), kind="ExternalInput").ap()
    f32 = _mybir.dt.float32
    ins["rel_ext"] = nc.dram_tensor("rel_ext", (8, 384), f32).ap()
    outs = {n: nc.dram_tensor(n, s, f32, kind="ExternalOutput").ap() for n, s in _OUTS}
    ins["gate_dram"] = nc.dram_tensor("gate_scratch", (NGB, P, P, GTOK), f32).ap()
    ins["act_dram"] = nc.dram_tensor("act_scratch", (NEXP // P, P, T), f32).ap()
    program(nc, ins, outs)
    r = _run(nc, [arrays], core_ids=[0])
    return tuple(r.results[0][n] for n, _ in _OUTS)
```
